# Optimizing a Trainium2 kernel written in Bass

```python
import jax
import jax.numpy as jnp
from jax import lax
import numpy as np

D_MODEL = 1024
BATCH = 1
SEQ = 256
DEPTH = 2
DEC_BATCH = 1
DEC_SEQ = 64
PAST_LEN = 512

CHUNK = 64
N_A_LAYERS = DEPTH // 2
N_B_LAYERS = DEPTH - N_A_LAYERS
N_DENSE = (DEPTH + 1) // 2
N_MOE = DEPTH // 2
GDN_HEADS = 8
GDN_DK = 128
GDN_DV = 128
GDN_QK_W = GDN_HEADS * GDN_DK
GDN_V_W = GDN_HEADS * GDN_DV
GDN_CONV_DIM = 2 * GDN_QK_W + GDN_V_W
GDN_IN_W = GDN_CONV_DIM + GDN_V_W + 2 * GDN_HEADS
CONV_W = 4
FOX_HEADS = 16
FOX_HEAD_DIM = D_MODEL // FOX_HEADS
FOX_W = FOX_HEADS * FOX_HEAD_DIM
KV_PROJ_W = 2 * FOX_W + FOX_HEADS
Q_BLOCK = 128
D_FF = 2816
N_EXPERTS = 8
TOP_K = 2
D_FF_EXPERT = 2816
NORM_EPS = 1e-6

kernel_name = "yoco_gdn_fox_stream_step"

def _rmsnorm(x, g):
    xf = x.astype(jnp.float32)
    y = xf * lax.rsqrt(jnp.mean(xf * xf, axis=-1, keepdims=True) + NORM_EPS)
    return (y * g.astype(jnp.float32)).astype(x.dtype)

def _l2norm(x):
    return x * lax.rsqrt(jnp.sum(x * x, axis=-1, keepdims=True) + 1e-6)

def _gated_delta_rule(q, k, v, g, beta, s0):
    B, T, H, _ = q.shape
    DV = v.shape[-1]
    C = min(CHUNK, T)
    N = T // C

    def blocks(a):
        return jnp.moveaxis(a.reshape((B, N, C, H) + a.shape[3:]), 3, 1)

    q, k, v, g, beta = blocks(q), blocks(k), blocks(v), blocks(g), blocks(beta)
    gc = jnp.cumsum(g, axis=-1)
    diff = gc[..., :, None] - gc[..., None, :]
    idx = jnp.arange(C)
    strict = idx[:, None] > idx[None, :]
    causal = idx[:, None] >= idx[None, :]
    kb = k * beta[..., None]
    lower = jnp.where(strict, jnp.einsum('bhncd,bhnsd->bhncs', kb, k) * jnp.exp(jnp.where(strict, diff, 0.0)), 0.0)
    m = lower + jnp.eye(C, dtype=jnp.float32)
    u = lax.linalg.triangular_solve(m, v * beta[..., None], left_side=True, lower=True, unit_diagonal=True)
    w = lax.linalg.triangular_solve(m, kb * jnp.exp(gc)[..., None], left_side=True, lower=True, unit_diagonal=True)
    a_qk = jnp.where(causal, jnp.einsum('bhncd,bhnsd->bhncs', q, k) * jnp.exp(jnp.where(causal, diff, 0.0)), 0.0)
    q_dec = q * jnp.exp(gc)[..., None]
    k_tail = k * jnp.exp(gc[..., -1:] - gc)[..., None]
    g_last = jnp.exp(gc[..., -1])

    def step(s, xs):
        q_c, k_c, u_c, w_c, a_c, gl = xs
        v_new = u_c - jnp.einsum('bhcd,bhde->bhce', w_c, s)
        o = jnp.einsum('bhcd,bhde->bhce', q_c, s) + jnp.einsum('bhcs,bhse->bhce', a_c, v_new)
        s = s * gl[..., None, None] + jnp.einsum('bhcd,bhce->bhde', k_c, v_new)
        return s, o

    xs = (jnp.moveaxis(q_dec, 2, 0), jnp.moveaxis(k_tail, 2, 0), jnp.moveaxis(u, 2, 0),
          jnp.moveaxis(w, 2, 0), jnp.moveaxis(a_qk, 2, 0), jnp.moveaxis(g_last, 2, 0))
    s_final, o = lax.scan(step, s0, xs)
    o = jnp.moveaxis(jnp.moveaxis(o, 0, 2), 1, 3).reshape(B, T, H, DV)
    return o, s_final

def _gdn_mixer(h, conv_ctx, s0, w_in, conv_w, a_log, dt_bias, o_gain, w_out):
    B, T, _ = h.shape
    proj = h @ w_in
    o1 = GDN_CONV_DIM
    o2 = o1 + GDN_V_W
    o3 = o2 + GDN_HEADS
    qkv, z, b_raw, a_raw = proj[..., :o1], proj[..., o1:o2], proj[..., o2:o3], proj[..., o3:]
    xp = jnp.concatenate([conv_ctx.astype(qkv.dtype), qkv], axis=1)
    conv = xp[:, 0:T] * conv_w[0]
    for i in range(1, CONV_W):
        conv = conv + xp[:, i:i + T] * conv_w[i]
    qkv_c = jax.nn.silu(conv).astype(jnp.float32)
    q = qkv_c[..., :GDN_QK_W].reshape(B, T, GDN_HEADS, GDN_DK)
    k = qkv_c[..., GDN_QK_W:2 * GDN_QK_W].reshape(B, T, GDN_HEADS, GDN_DK)
    v = qkv_c[..., 2 * GDN_QK_W:].reshape(B, T, GDN_HEADS, GDN_DV)
    q = _l2norm(q) * (GDN_DK ** -0.5)
    k = _l2norm(k)
    beta = jax.nn.sigmoid(b_raw.astype(jnp.float32))
    g = -jnp.exp(a_log.astype(jnp.float32)) * jax.nn.softplus(a_raw.astype(jnp.float32) + dt_bias.astype(jnp.float32))
    o, s = _gated_delta_rule(q, k, v, g, beta, s0.astype(jnp.float32))
    o = _rmsnorm(o, o_gain) * jax.nn.silu(z.astype(jnp.float32).reshape(B, T, GDN_HEADS, GDN_DV))
    y = o.reshape(B, T, GDN_V_W).astype(h.dtype) @ w_out
    return y, xp[:, -(CONV_W - 1):], s

def _fox_attention(q, k, v, f_q, f_k, q_off):
    B, Tq, H, hd = q.shape
    Tk = k.shape[1]
    blk = min(Q_BLOCK, Tq)
    nb = Tq // blk
    q_blocks = jnp.moveaxis(q.reshape(B, nb, blk, H, hd), 1, 0)
    fq_blocks = jnp.moveaxis(f_q.reshape(B, nb, blk, H), 1, 0)
    f_k_t = jnp.swapaxes(f_k, 1, 2)
    k_pos = jnp.arange(Tk)
    scale = hd ** -0.5

    def one_block(args):
        q_b, fq_b, start = args
        s = jnp.einsum('bqhd,bkhd->bhqk', q_b, k, preferred_element_type=jnp.float32) * scale
        s = s + (jnp.swapaxes(fq_b, 1, 2)[..., :, None] - f_k_t[:, :, None, :])
        q_pos = q_off + start + jnp.arange(blk)
        s = jnp.where(k_pos[None, :] <= q_pos[:, None], s, -jnp.inf)
        p = jax.nn.softmax(s, axis=-1)
        return jnp.einsum('bhqk,bkhd->bqhd', p.astype(v.dtype), v)

    o = lax.map(one_block, (q_blocks, fq_blocks, jnp.arange(nb) * blk))
    return jnp.moveaxis(o, 0, 1).reshape(B, Tq, H, hd)

def _swiglu(h, w_gate, w_up, w_down):
    return (jax.nn.silu(h @ w_gate) * (h @ w_up)) @ w_down

def _moe(h, router_w, router_b, w_gate, w_up, w_down):
    logits = (h @ router_w).astype(jnp.float32) + router_b.astype(jnp.float32)
    top_v, top_i = lax.top_k(logits, TOP_K)
    wts = jax.nn.softmax(top_v, axis=-1)
    gate = jnp.sum(jax.nn.one_hot(top_i, N_EXPERTS, dtype=jnp.float32) * wts[..., None], axis=-2)
    y = jnp.zeros(h.shape, h.dtype)
    for e in range(N_EXPERTS):
        y = y + gate[..., e:e + 1].astype(h.dtype) * _swiglu(h, w_gate[e], w_up[e], w_down[e])
    return y

def _trunk(x, c, conv_ctx, s0, past_k, past_v, past_logf, p):
    B, T, _ = x.shape
    sc = jax.nn.silu(c)
    conv_out, s_out = [], []
    k_new = v_new = logf_new = None
    k_all = v_all = f_q = f_k = None
    q_off = 0
    for l in range(DEPTH):
        mod = (sc @ p['ada_w'][l] + p['ada_b'][l])[:, None, :]
        sh_m, sc_m, gt_m, sh_f, sc_f, gt_f = jnp.split(mod, 6, axis=-1)
        h = _rmsnorm(x, p['pre_mix_g'][l]) * (1 + sc_m) + sh_m
        if l < N_A_LAYERS:
            y, ctx, s = _gdn_mixer(h, conv_ctx[:, l], s0[:, l], p['gdn_w_in'][l], p['gdn_conv_w'][l],
                                   p['gdn_a_log'][l], p['gdn_dt_bias'][l], p['gdn_o_gain'][l], p['gdn_w_out'][l])
            conv_out.append(ctx)
            s_out.append(s)
        else:
            j = l - N_A_LAYERS
            q = (h @ p['fox_w_q'][j]).reshape(B, T, FOX_HEADS, FOX_HEAD_DIM)
            o = _fox_attention(q, k_all, v_all, f_q, f_k, q_off)
            y = o.reshape(B, T, FOX_W) @ p['fox_w_o'][j]
        x = x + gt_m * _rmsnorm(y, p['post_mix_g'][l])
        h = _rmsnorm(x, p['pre_ffn_g'][l]) * (1 + sc_f) + sh_f
        if l % 2 == 0:
            i = l // 2
            y = _swiglu(h, p['ffn_w_gate'][i], p['ffn_w_up'][i], p['ffn_w_down'][i])
        else:
            i = l // 2
            y = _moe(h, p['moe_router_w'][i], p['moe_router_b'][i], p['moe_w_gate'][i],
                     p['moe_w_up'][i], p['moe_w_down'][i])
        x = x + gt_f * _rmsnorm(y, p['post_ffn_g'][l])
        if l == N_A_LAYERS - 1:
            kvm = (sc @ p['kv_ada_w'] + p['kv_ada_b'])[:, None, :]
            sh_kv, sc_kv = jnp.split(kvm, 2, axis=-1)
            hk = _rmsnorm(x, p['kv_norm_g']) * (1 + sc_kv) + sh_kv
            kvp = hk @ p['kv_w']
            k_new = kvp[..., :FOX_W].reshape(B, T, FOX_HEADS, FOX_HEAD_DIM)
            v_new = kvp[..., FOX_W:2 * FOX_W].reshape(B, T, FOX_HEADS, FOX_HEAD_DIM)
            logf_new = jax.nn.log_sigmoid(kvp[..., 2 * FOX_W:].astype(jnp.float32) + p['kv_b_f'].astype(jnp.float32))
            if past_k is None:
                k_all, v_all, logf_all, q_off = k_new, v_new, logf_new, 0
            else:
                k_all = jnp.concatenate([past_k.astype(k_new.dtype), k_new], axis=1)
                v_all = jnp.concatenate([past_v.astype(v_new.dtype), v_new], axis=1)
                logf_all = jnp.concatenate([past_logf.astype(jnp.float32), logf_new], axis=1)
                q_off = past_k.shape[1]
            f_k = jnp.cumsum(logf_all, axis=1)
            f_q = f_k[:, q_off:]
    return x, k_new, v_new, logf_new, jnp.stack(s_out, axis=1), jnp.stack(conv_out, axis=1)

def setup_inputs(seed: int = 0) -> dict:
    key = jax.random.key(seed)
    ks = list(jax.random.split(key, 48))
    cnt = [0]

    def nk():
        cnt[0] += 1
        return ks[cnt[0] - 1]

    def nrm(shape, scale):
        return jax.random.normal(nk(), shape, jnp.float32) * scale

    D = D_MODEL
    dt = jnp.exp(jax.random.uniform(nk(), (N_A_LAYERS, GDN_HEADS), jnp.float32, np.log(1e-3), np.log(1e-1)))
    return {
        'x_prompt': nrm((BATCH, SEQ, D), 1.0),
        'x_sample': nrm((DEC_BATCH, DEC_SEQ, D), 1.0),
        'c_prompt': nrm((BATCH, D), 1.0),
        'c_sample': nrm((DEC_BATCH, D), 1.0),
        'cache_k': nrm((DEC_BATCH, PAST_LEN, FOX_HEADS, FOX_HEAD_DIM), 1.0),
        'cache_v': nrm((DEC_BATCH, PAST_LEN, FOX_HEADS, FOX_HEAD_DIM), 1.0),
        'cache_logf': jax.nn.log_sigmoid(2.5 + nrm((DEC_BATCH, PAST_LEN, FOX_HEADS), 1.0)),
        'state_delta': nrm((DEC_BATCH, N_A_LAYERS, GDN_HEADS, GDN_DK, GDN_DV), 0.1),
        'state_conv': nrm((DEC_BATCH, N_A_LAYERS, CONV_W - 1, GDN_CONV_DIM), 1.0),
        'ada_w': nrm((DEPTH, D, 6 * D), 0.5 * D ** -0.5),
        'ada_b': nrm((DEPTH, 6 * D), 0.02),
        'pre_mix_g': 1.0 + nrm((DEPTH, D), 0.05),
        'post_mix_g': 1.0 + nrm((DEPTH, D), 0.05),
        'pre_ffn_g': 1.0 + nrm((DEPTH, D), 0.05),
        'post_ffn_g': 1.0 + nrm((DEPTH, D), 0.05),
        'gdn_w_in': nrm((N_A_LAYERS, D, GDN_IN_W), D ** -0.5),
        'gdn_conv_w': nrm((N_A_LAYERS, CONV_W, GDN_CONV_DIM), CONV_W ** -0.5),
        'gdn_a_log': jnp.log(jax.random.uniform(nk(), (N_A_LAYERS, GDN_HEADS), jnp.float32, 1.0, 16.0)),
        'gdn_dt_bias': dt + jnp.log(-jnp.expm1(-dt)),
        'gdn_o_gain': 1.0 + nrm((N_A_LAYERS, GDN_DV), 0.05),
        'gdn_w_out': nrm((N_A_LAYERS, GDN_V_W, D), GDN_V_W ** -0.5),
        'kv_norm_g': 1.0 + nrm((D,), 0.05),
        'kv_ada_w': nrm((D, 2 * D), 0.5 * D ** -0.5),
        'kv_ada_b': nrm((2 * D,), 0.02),
        'kv_w': nrm((D, KV_PROJ_W), D ** -0.5),
        'kv_b_f': jax.random.uniform(nk(), (FOX_HEADS,), jnp.float32, 1.0, 4.0),
        'fox_w_q': nrm((N_B_LAYERS, D, FOX_W), D ** -0.5),
        'fox_w_o': nrm((N_B_LAYERS, FOX_W, D), FOX_W ** -0.5),
        'ffn_w_gate': nrm((N_DENSE, D, D_FF), D ** -0.5),
        'ffn_w_up': nrm((N_DENSE, D, D_FF), D ** -0.5),
        'ffn_w_down': nrm((N_DENSE, D_FF, D), D_FF ** -0.5),
        'moe_router_w': nrm((N_MOE, D, N_EXPERTS), D ** -0.5),
        'moe_router_b': nrm((N_MOE, N_EXPERTS), 0.01),
        'moe_w_gate': nrm((N_MOE, N_EXPERTS, D, D_FF_EXPERT), D ** -0.5),
        'moe_w_up': nrm((N_MOE, N_EXPERTS, D, D_FF_EXPERT), D ** -0.5),
        'moe_w_down': nrm((N_MOE, N_EXPERTS, D_FF_EXPERT, D), D_FF_EXPERT ** -0.5),
    }

def reference(x_prompt, x_sample, c_prompt, c_sample, cache_k, cache_v, cache_logf, state_delta, state_conv,
              ada_w, ada_b, pre_mix_g, post_mix_g, pre_ffn_g, post_ffn_g,
              gdn_w_in, gdn_conv_w, gdn_a_log, gdn_dt_bias, gdn_o_gain, gdn_w_out,
              kv_norm_g, kv_ada_w, kv_ada_b, kv_w, kv_b_f, fox_w_q, fox_w_o,
              ffn_w_gate, ffn_w_up, ffn_w_down,
              moe_router_w, moe_router_b, moe_w_gate, moe_w_up, moe_w_down):
    p = {
        'ada_w': ada_w, 'ada_b': ada_b, 'pre_mix_g': pre_mix_g, 'post_mix_g': post_mix_g,
        'pre_ffn_g': pre_ffn_g, 'post_ffn_g': post_ffn_g,
        'gdn_w_in': gdn_w_in, 'gdn_conv_w': gdn_conv_w, 'gdn_a_log': gdn_a_log, 'gdn_dt_bias': gdn_dt_bias,
        'gdn_o_gain': gdn_o_gain, 'gdn_w_out': gdn_w_out,
        'kv_norm_g': kv_norm_g, 'kv_ada_w': kv_ada_w, 'kv_ada_b': kv_ada_b, 'kv_w': kv_w, 'kv_b_f': kv_b_f,
        'fox_w_q': fox_w_q, 'fox_w_o': fox_w_o,
        'ffn_w_gate': ffn_w_gate, 'ffn_w_up': ffn_w_up, 'ffn_w_down': ffn_w_down,
        'moe_router_w': moe_router_w, 'moe_router_b': moe_router_b, 'moe_w_gate': moe_w_gate,
        'moe_w_up': moe_w_up, 'moe_w_down': moe_w_down,
    }
    bp = x_prompt.shape[0]
    conv0 = jnp.zeros((bp, N_A_LAYERS, CONV_W - 1, GDN_CONV_DIM), x_prompt.dtype)
    s00 = jnp.zeros((bp, N_A_LAYERS, GDN_HEADS, GDN_DK, GDN_DV), jnp.float32)
    y_prompt, k_p, v_p, f_p, d_p, c_p = _trunk(x_prompt, c_prompt, conv0, s00, None, None, None, p)
    y_sample, k_s, v_s, f_s, d_s, c_s = _trunk(x_sample, c_sample, state_conv, state_delta,
                                              cache_k, cache_v, cache_logf, p)
    return (y_prompt, y_sample, k_p, v_p, f_p, d_p, c_p, k_s, v_s, f_s, d_s, c_s)


_drawn_inputs = setup_inputs


def setup_inputs(seed=0):
    import zlib

    import numpy as np

    out = dict(_drawn_inputs(seed))
    spreads = {}
    factors = {'cache_logf': 3.002, 'moe_router_b': 3.514}
    for name, (base, spread) in spreads.items():
        noise = np.random.default_rng([zlib.crc32(name.encode()), seed]).standard_normal(out[name].shape)
        drawn = base * np.exp(spread * noise) if base else spread * noise
        out[name] = jnp.asarray(drawn.astype(out[name].dtype))
    for name, factor in factors.items():
        out[name] = (out[name] * factor).astype(out[name].dtype)
    return out
```

```python
import numpy as np
import concourse.bass as bass
import concourse.mybir as mybir
from concourse.alu_op_type import AluOpType as ALU
from contextlib import ExitStack

F32 = mybir.dt.float32
F32R = mybir.dt.float32r
I32 = mybir.dt.int32
U32 = mybir.dt.uint32
ACT = mybir.ActivationFunctionType
AX = mybir.AxisListType

P = 128
D = 1024
KT = D // P
TP, TS = 256, 64
T = TP + TS
STREAMS = ((0, TP), (TP, TS))
TOKEN_TILES = ((0, 128), (128, 128), (256, 64))
PAST = 512
CHUNK = 64
NCH = T // CHUNK
H, DK = 8, 128
QKV_T = 3 * H
GDN_IN = 4 * D + 2 * H
CONV = 4
FH, FD = 16, 64
FF = 2816
FT = FF // P
NE = 8
EPS = 1e-6
SLAB = 2048
RAW = 6
SPL = 3
AHEAD = 2
MASKED = -1e30
N_ADA = 6 * KT


class Serial:

    def __init__(self, sem):
        self.sem, self.n = sem, 0

    def on(self, eng):
        def run(ins):
            ins.then_inc(self.sem, 1)
            self.n += 1
            eng.wait_ge(self.sem, self.n)
        return run


def hbm_inputs(nc, arrays):
    return {name: nc.dram_tensor(f"in_{name}", a.shape, F32, kind="ExternalInput").ap() for name, a in arrays.items()}


def hbm_outputs(nc):
    out, order = {}, []
    shapes = {"y": (D,), "k": (FH, FD), "v": (FH, FD), "logf": (FH,)}
    for s, n in enumerate((TP, TS)):
        for name in ("y", "k", "v", "logf", "delta", "conv"):
            shape = (1, 1, H, DK, DK) if name == "delta" else (1, 1, CONV - 1, QKV_T * P) if name == "conv" else \
                (1, n) + shapes[name]
            out.setdefault(name, []).append(nc.dram_tensor(f"out_{name}{s}", shape, F32, kind="ExternalOutput").ap())
    return out


UP_SLABS, DOWN_SLABS = 2 * FF // 256, FF // 256
EXPERT_SLABS = UP_SLABS + DOWN_SLABS


def moe_parts(i, e, j):
    def of(name):
        w = i[name][0]
        return (w[e] if isinstance(e, int) else w[bass.ds(e, 1)].rearrange("o r c -> (o r) c")).rearrange(
            "(k p) n -> p k n", p=P)
    if j < UP_SLABS:
        ks, cs = slice(4 * (j % 2), 4 * (j % 2) + 4), slice(j // 2 * 256, j // 2 * 256 + 256)
        return [(0, 256, 4, of("moe_w_gate")[:, ks, cs]), (256, 256, 4, of("moe_w_up")[:, ks, cs])]
    down = i["moe_w_down"][0].rearrange("e (k p) n -> p (e k) n", p=P)
    return [(0, D, 2, down[:, bass.ds(e * FT + 2 * (j - UP_SLABS), 2), :])]


def slab_list(i):
    slabs, first = [], {}

    def cols(w, c0, n, kts=KT, k0=0):
        return w.rearrange("(k p) n -> p k n", p=P)[:, k0:k0 + kts, c0:c0 + n]

    def full(name, w, c0, c1, kind):
        first.setdefault(name, len(slabs))
        for c in range(c0, c1, 256):
            slabs.append((kind, [(0, 256, KT, cols(w, c, 256))]))

    ada = i["ada_w"]
    full("ada_mix0", ada[0], 0, 2 * D, "raw")
    full("w_in", i["gdn_w_in"][0], 0, 4 * D, "split")
    full("ada_rest", ada[0], 2 * D, 6 * D, "raw")
    full("ada_rest", i["kv_ada_w"], 0, 2 * D, "raw")
    full("ada_rest", ada[1], 0, 6 * D, "raw")
    full("w_out", i["gdn_w_out"][0], 0, D, "split")
    first["ffn_up"] = len(slabs)
    for f in range(FT):
        slabs.append(("split", [(0, 128, KT, cols(i["ffn_w_gate"][0], f * P, P)),
                                (128, 128, KT, cols(i["ffn_w_up"][0], f * P, P))]))
    first["ffn_down"] = len(slabs)
    for c in range(0, D, 256):
        for k0, nk in ((0, 8), (8, 8), (16, 6)):
            slabs.append(("split", [(0, 256, nk, cols(i["ffn_w_down"][0], c, 256, nk, k0))]))
    full("kv_w", i["kv_w"], 0, D, "split")
    full("kv_w2", i["kv_w"], D, 2 * D, "split")
    full("w_q", i["fox_w_q"][0], 0, D, "split")
    full("w_o", i["fox_w_o"][0], 0, D, "split")
    first["moe"] = len(slabs)
    for j in range(RAW):
        slabs.append(("split", moe_parts(i, 0, j)))
    return slabs, first


class Kernel:

    def __init__(self, nc, ctx, i, o):
        self.nc, self.ctx, self.i, self.o = nc, ctx, i, o
        self.slabs, self.first = slab_list(i)
        split = 0
        self.order = []
        raws = 0
        for kind, _ in self.slabs:
            self.order.append(split if kind == "split" else raws)
            split += kind == "split"
            raws += kind == "raw"
        self.moe_slab, self.moe_split = len(self.slabs), split
        sb = self.sb
        self.raw = sb("raw", [P, RAW, SLAB])
        self.w_hi = sb("w_hi", [P, SPL, SLAB], F32R)
        self.w_lo = sb("w_lo", [P, SPL, SLAB], F32R)
        self.xT = sb("xT", [P, KT, T])
        self.yT = sb("yT", [P, KT, T])
        self.ident = sb("ident", [P, P])
        self.ones = sb("ones", [P, P])
        self.tri_incl = sb("tri_incl", [P, P])
        self.tri_strict = sb("tri_strict", [P, P])
        self.mod = sb("mod", [P, 2 * N_ADA + 2 * KT, 2])
        self.vec_a = sb("vec_a", [P, 112])
        self.vec_b = sb("vec_b", [P, 89])
        self.silu_c = sb("silu_c", [P, KT, 2])
        self.coef = sb("coef", [P, KT, 2])
        self.ps = [ctx.enter_context(nc.psum_tensor(f"bank{b}", [P, 512], F32)) for b in range(8)]
        self.raw_full = [self.sem(f"raw_full{s}") for s in range(RAW)]
        self.raw_split = self.sem("raw_split")
        self.hi_ready = self.sem("hi_ready")
        self.raw_read = self.sem("raw_read")
        self.split_read = self.sem("split_read")
        self.dve_chain = Serial(self.sem("dve_chain"))
        self.act_chain = Serial(self.sem("act_chain"))
        self.pool_chain = Serial(self.sem("pool_chain"))
        self.norm_sems = [self.sem(f"norm_{n}") for n in ("squared", "part", "inverse", "rstd", "scaled")]
        self.norm_parts = [self.sem("norm_hi"), self.sem("norm_lo")]
        self.norm_uses = self.norm_part_uses = 0
        self.stores = [self.sem("stores")]
        self.n_store = [0]
        self.GAINS = {"pre_mix": 0, "post_mix": 16, "pre_ffn": 32, "post_ffn": 48, "kv": 64}

    def sb(self, name, shape, dt=F32):
        return self.ctx.enter_context(self.nc.sbuf_tensor(name, shape, dt))

    def sem(self, name):
        return self.ctx.enter_context(self.nc.semaphore(name))

    def slab_view(self, t, slot, words, cols, kts, width):
        return t[:, slot, 0:kts * width].rearrange("p (k n) -> p k n", k=kts)[:, :, words:words + cols]

    def load(self, sp, n):
        if n >= len(self.slabs):
            return
        if n >= RAW:
            kind, k = self.slabs[n - RAW][0], self.order[n - RAW]
            sp.wait_ge(self.raw_split if kind == "split" else self.raw_read, k + 1)
        self.loaded = n
        for words, cols, kts, src in self.slabs[n][1]:
            width = sum(part[1] for part in self.slabs[n][1])
            sp.dma_start(self.slab_view(self.raw, n % RAW, words, cols, kts, width), src).then_inc(self.raw_full[n % RAW], 16)

    def full_count(self, n):
        return 16 * sum(len(self.slabs[m][1]) for m in range(n % RAW, n + 1, RAW))

    def used(self, n):
        _, cols, kts, _ = self.slabs[n][1][-1]
        return kts * sum(part[1] for part in self.slabs[n][1])

    def split_hi(self, act, n):
        m, words = self.order[n], self.used(n)
        act.wait_ge(self.raw_full[n % RAW], self.full_count(n))
        if m >= SPL:
            act.wait_ge(self.split_read, m - SPL + 1)
        act.activation(self.w_hi[:, m % SPL, 0:words], self.raw[:, n % RAW, 0:words], ACT.Copy).then_inc(self.hi_ready, 1)

    def split_lo(self, dve, n):
        m, words = self.order[n], self.used(n)
        dve.wait_ge(self.raw_full[n % RAW], self.full_count(n))
        dve.wait_ge(self.hi_ready, m + 1)
        dve.tensor_tensor(self.w_lo[:, m % SPL, 0:words], self.raw[:, n % RAW, 0:words],
                          self.w_hi[:, m % SPL, 0:words], ALU.subtract).then_inc(self.raw_split, 1)

    def ahead_hi(self, act, upto):
        while self.next_hi <= upto and self.next_hi < len(self.slabs) and self.slabs[self.next_hi][0] == "split":
            self.split_hi(act, self.next_hi)
            self.next_hi += 1

    def ahead_lo(self, dve, upto):
        while self.next_lo <= upto and self.next_lo < len(self.slabs) and self.slabs[self.next_lo][0] == "split":
            self.split_lo(dve, self.next_lo)
            self.next_lo += 1

    def start_splits(self, n):
        self.next_hi = self.next_lo = n

    def three(self, pe, out, w_hi, w_lo, x_hi, x_lo, start, stop):
        pe.matmul(out, w_hi, x_hi, start=start, stop=False)
        pe.matmul(out, w_hi, x_lo, start=False, stop=False)
        return pe.matmul(out, w_lo, x_hi, start=False, stop=stop)

    def store(self, eng, q, dst, src):
        eng.dma_start(dst, src).then_inc(self.stores[q], 16)
        self.n_store[q] += 16

    def gain(self, name, layer=0):
        c = self.GAINS[name] + KT * layer
        return self.vec_b[:, c:c + KT]

    def mod_tiles(self, layer, which):
        c = which * KT + (layer * (N_ADA + 2 * KT))
        return self.mod[:, c:c + KT, :]


SH_M, SC_M, GT_M, SH_F, SC_F, GT_F = range(6)
KV_MOD = N_ADA


def setup_phase(k):
    nc, i = k.nc, k.i
    k.wba = k.sb("wba", [P, KT, 2 * H])
    k.wlf = k.sb("wlf", [P, KT, FH])
    k.w_router = k.sb("w_router", [P, KT, NE])
    k.b_router = k.sb("b_router", [P, NE])
    k.b_forget = k.sb("b_forget", [P, FH])
    k.a_log = k.sb("a_log", [CHUNK, H])
    k.dt_bias = k.sb("dt_bias", [CHUNK, H])
    k.conv_cols = k.sb("conv_cols", [P, QKV_T, 7])
    with nc.sbuf_tensor("x_tok", [P, 3, D], F32) as x_tok, \
            nc.sbuf_tensor("rows_a", [112, P], F32) as rows_a, \
            nc.sbuf_tensor("rows_b", [89, P], F32) as rows_b, \
            nc.sbuf_tensor("conv_rows", [7, QKV_T * P], F32) as conv_rows, \
            nc.semaphore("small_in") as small_in, nc.semaphore("const_ready") as const_ready, \
            nc.semaphore("turned") as turned, nc.semaphore("copied") as copied, nc.Block() as block:
        loads = []

        def rows(dst, src):
            loads.append((dst, src))

        for t in range(2):
            rows(x_tok[:, t, :], i["x_prompt"][0, t * P:(t + 1) * P, :])
        rows(x_tok[0:TS, 2, :], i["x_sample"][0])
        rows(rows_a[0:48], i["ada_b"][0].rearrange("(r c) -> r c", c=P))
        rows(rows_a[48:64], i["kv_ada_b"].rearrange("(r c) -> r c", c=P))
        rows(rows_a[64:112], i["ada_b"][1].rearrange("(r c) -> r c", c=P))
        for n, name in enumerate(("pre_mix_g", "post_mix_g", "pre_ffn_g", "post_ffn_g")):
            rows(rows_b[16 * n:16 * n + 16], i[name].rearrange("l (r c) -> (l r) c", c=P))
        rows(rows_b[64:72], i["kv_norm_g"].rearrange("(r c) -> r c", c=P))
        rows(rows_b[72:73], i["gdn_o_gain"])
        rows(rows_b[73:81], i["c_prompt"].rearrange("o (r c) -> (o r) c", c=P))
        rows(rows_b[81:89], i["c_sample"].rearrange("o (r c) -> (o r) c", c=P))
        rows(conv_rows[0:4], i["gdn_conv_w"][0])
        rows(conv_rows[4:7], i["state_conv"][0, 0])
        rows(k.wba[:], i["gdn_w_in"][0].rearrange("(k p) n -> p k n", p=P)[:, :, 4 * D:GDN_IN])
        rows(k.wlf[:], i["kv_w"].rearrange("(k p) n -> p k n", p=P)[:, :, 2 * D:2 * D + FH])
        rows(k.w_router[:], i["moe_router_w"][0].rearrange("(k p) n -> p k n", p=P))
        rows(k.b_router[:], i["moe_router_b"][0].partition_broadcast(P))
        rows(k.b_forget[:], i["kv_b_f"].partition_broadcast(P))
        rows(k.a_log[:], i["gdn_a_log"][0].partition_broadcast(CHUNK))
        rows(k.dt_bias[:], i["gdn_dt_bias"][0].partition_broadcast(CHUNK))
        all_in = 16 * len(loads)
        turns = []
        for t, (t0, nt) in enumerate(TOKEN_TILES):
            for half in range(2):
                ins = [x_tok[0:nt, t, (4 * half + q) * P:(4 * half + q + 1) * P] for q in range(4)]
                turns.append((ins, nt, k.xT[:, 4 * half:4 * half + 4, t0:t0 + nt]))
        turns.append(([rows_a[:]], 112, k.vec_a[:].unsqueeze(1)))
        turns.append(([rows_b[:]], 89, k.vec_b[:].unsqueeze(1)))
        turns.append(([conv_rows[:, q * P:(q + 1) * P] for q in range(QKV_T)], 7, k.conv_cols[:]))

        @block.sync
        def _(sp):
            for n in range(RAW):
                k.load(sp, n)

        @block.gpsimd
        def _(pool):
            run = k.pool_chain.on(pool)
            pool.memset(k.ones[:], 1.0)
            pool.memset(k.ident[:], 0.0)
            pool.memset(k.tri_strict[:], 1.0)
            run(pool.memset(k.tri_incl[:], 1.0))
            pool.affine_select(out=k.ident[:], in_=k.ident[:], compare_op=ALU.not_equal, fill=1.0, base=0,
                               pattern=[[-1, P]], channel_multiplier=1)
            pool.affine_select(out=k.tri_incl[:], in_=k.tri_incl[:], compare_op=ALU.is_ge, fill=0.0, base=0,
                               pattern=[[1, P]], channel_multiplier=-1)
            pool.affine_select(out=k.tri_strict[:], in_=k.tri_strict[:], compare_op=ALU.is_gt, fill=0.0, base=0,
                               pattern=[[1, P]], channel_multiplier=-1).then_inc(const_ready, 1)

        @block.tensor
        def _(pe):
            pe.wait_ge(const_ready, 1)
            pe.wait_ge(small_in, all_in)
            for n, (ins, width, _) in enumerate(turns):
                if n >= 8:
                    pe.wait_ge(copied, n - 7)
                for q, src in enumerate(ins):
                    last = pe.transpose(k.ps[n % 8][:, q * width:(q + 1) * width], src,
                                        k.ident[0:src.shape[0], 0:src.shape[0]])
                last.then_inc(turned, 1)

        @block.scalar
        def _(act):
            for dst, src in loads:
                act.dma_start(dst, src).then_inc(small_in, 16)
            act.wait_ge(copied, len(turns))
            for s, c in ((0, 73), (1, 81)):
                act.activation(k.silu_c[:, :, s], k.vec_b[:, c:c + KT], ACT.Silu)

        @block.vector
        def _(dve):
            for n, (ins, width, dst) in enumerate(turns):
                dve.wait_ge(turned, n + 1)
                src = k.ps[n % 8][:, 0:len(ins) * width].rearrange("p (q n) -> p q n", n=width)
                dve.tensor_copy(dst, src).then_inc(copied, 1)


def ada_slab(k, pe, n, col, psum):
    pe.wait_ge(k.raw_full[n % RAW], k.full_count(n))
    w = k.slab_view(k.raw, n % RAW, 0, 256, KT, 256)
    for half in range(2):
        for kt in range(KT):
            last = pe.matmul(psum[:, col + 2 * half:col + 2 * half + 2], w[:, kt, half * P:(half + 1) * P],
                             k.silu_c[:, kt, :], start=(kt == 0), stop=(kt == KT - 1))
    last.then_inc(k.raw_read, 1)
    return last


def ada_phase(k):
    nc, n0 = k.nc, k.first["ada_mix0"]
    with nc.Block() as block:
        @block.sync
        def _(sp):
            for n in range(n0, n0 + 8):
                k.load(sp, n + RAW)

        @block.tensor
        def _(pe):
            for j in range(8):
                ada_slab(k, pe, n0 + j, 4 * j, k.ps[0])

        @block.vector
        def _(dve):
            dve.wait_ge(k.raw_read, 8)
            dve.tensor_tensor(k.mod[:, 0:16, :], k.ps[0][:, 0:32].rearrange("p (t s) -> p t s", s=2),
                              k.vec_a[:, 0:16].unsqueeze(2).to_broadcast([P, 16, 2]), ALU.add)


def norm_phase(k, src, gain, scale, shift, hi, lo, h32=None, name=""):
    nc = k.nc
    with nc.sbuf_tensor(f"rstd{name}", [P, T], F32) as rstd, nc.sbuf_tensor(f"sq{name}", [P, 2, T], F32) as sq, \
            nc.sbuf_tensor(f"tmp{name}", [P, 2, T], F32) as tmp, nc.Block() as block:
        squared, part, inv, rstd_ready, scaled = k.norm_sems
        hi_done, lo_done = k.norm_parts
        uses, part_uses = k.norm_uses, k.norm_part_uses
        k.norm_uses, k.norm_part_uses = uses + 1, part_uses + 1

        @block.scalar
        def _(act):
            for kt in range(KT):
                if kt >= 2:
                    act.wait_ge(part, uses * KT + kt - 1)
                act.activation(sq[:, kt % 2, :], src[:, kt, :], ACT.Square).then_inc(squared, 1)
            act.wait_ge(inv, uses + 1)
            act.activation(rstd[:], rstd[:], ACT.Sqrt).then_inc(rstd_ready, 1)
            for kt in range(KT):
                act.wait_ge(scaled, uses * KT + kt + 1)
                for s, (c0, n) in enumerate(STREAMS):
                    last = act.activation(hi[:, kt, c0:c0 + n], tmp[:, kt % 2, c0:c0 + n], ACT.Identity,
                                          bias=shift[:, kt, s:s + 1])
                last.then_inc(hi_done, 1)

        @block.tensor
        def _(pe):
            for kt in range(KT):
                pe.wait_ge(squared, uses * KT + kt + 1)
                pe.matmul(k.ps[7][:, 0:T], k.ones[:], sq[:, kt % 2, :], start=(kt == 0),
                          stop=(kt == KT - 1)).then_inc(part, 1)

        @block.vector
        def _(dve):
            run = k.dve_chain.on(dve)
            run(dve.tensor_scalar(k.coef[:], scale, 1.0, None, ALU.add))
            run(dve.tensor_tensor(k.coef[:], k.coef[:], gain.unsqueeze(2).to_broadcast([P, KT, 2]), ALU.mult))
            dve.wait_ge(part, uses * KT + KT)
            run(dve.tensor_scalar(rstd[:], k.ps[7][:, 0:T], 1.0 / D, EPS, ALU.mult, ALU.add))
            dve.reciprocal(rstd[:], rstd[:]).then_inc(inv, 1)
            dve.wait_ge(rstd_ready, uses + 1)

            def low(kt):
                dve.wait_ge(hi_done, part_uses * KT + kt + 1)
                for s, (c0, n) in enumerate(STREAMS):
                    if h32 is not None:
                        dve.tensor_scalar(h32[:, kt, c0:c0 + n], tmp[:, kt % 2, c0:c0 + n], shift[:, kt, s:s + 1],
                                          None, ALU.add)
                    last = dve.scalar_tensor_tensor(lo[:, kt, c0:c0 + n], tmp[:, kt % 2, c0:c0 + n],
                                                    shift[:, kt, s:s + 1], hi[:, kt, c0:c0 + n], ALU.add, ALU.subtract)
                last.then_inc(lo_done, 1)

            for kt in range(KT):
                if kt >= 2:
                    dve.wait_ge(lo_done, part_uses * KT + kt - 1)
                for s, (c0, n) in enumerate(STREAMS):
                    last = dve.scalar_tensor_tensor(tmp[:, kt % 2, c0:c0 + n], src[:, kt, c0:c0 + n],
                                                    k.coef[:, kt, s:s + 1], rstd[:, c0:c0 + n], ALU.mult, ALU.mult)
                last.then_inc(scaled, 1)
                if kt >= 1:
                    low(kt - 1)
            low(KT - 1)


def residual_phase(k, gate, gain, name):
    nc = k.nc
    with nc.sbuf_tensor(f"y_inv{name}", [P, T], F32) as rstd, nc.sbuf_tensor(f"y_sq{name}", [P, 2, T], F32) as sq, \
            nc.Block() as block:
        squared, part, inv, rstd_ready, scaled = k.norm_sems
        uses = k.norm_uses
        k.norm_uses = uses + 1

        @block.scalar
        def _(act):
            for kt in range(KT):
                if kt >= 2:
                    act.wait_ge(part, uses * KT + kt - 1)
                act.activation(sq[:, kt % 2, :], k.yT[:, kt, :], ACT.Square).then_inc(squared, 1)
            act.wait_ge(inv, uses + 1)
            act.activation(rstd[:], rstd[:], ACT.Sqrt).then_inc(rstd_ready, 1)

        @block.tensor
        def _(pe):
            for kt in range(KT):
                pe.wait_ge(squared, uses * KT + kt + 1)
                pe.matmul(k.ps[7][:, 0:T], k.ones[:], sq[:, kt % 2, :], start=(kt == 0),
                          stop=(kt == KT - 1)).then_inc(part, 1)

        @block.vector
        def _(dve):
            run = k.dve_chain.on(dve)
            run(dve.tensor_tensor(k.coef[:], gate, gain.unsqueeze(2).to_broadcast([P, KT, 2]), ALU.mult))
            dve.wait_ge(part, uses * KT + KT)
            run(dve.tensor_scalar(rstd[:], k.ps[7][:, 0:T], 1.0 / D, EPS, ALU.mult, ALU.add))
            dve.reciprocal(rstd[:], rstd[:]).then_inc(inv, 1)
            dve.wait_ge(rstd_ready, uses + 1)
            for kt in range(KT):
                for s, (c0, n) in enumerate(STREAMS):
                    last = dve.scalar_tensor_tensor(k.yT[:, kt, c0:c0 + n], k.yT[:, kt, c0:c0 + n],
                                                    k.coef[:, kt, s:s + 1], rstd[:, c0:c0 + n], ALU.mult, ALU.mult)
                last.then_inc(scaled, 1)
                if kt >= 1:
                    dve.wait_ge(scaled, uses * KT + kt)
                    dve.tensor_tensor(k.xT[:, kt - 1, :], k.xT[:, kt - 1, :], k.yT[:, kt - 1, :], ALU.add)
            dve.wait_ge(scaled, uses * KT + KT)
            dve.tensor_tensor(k.xT[:, KT - 1, :], k.xT[:, KT - 1, :], k.yT[:, KT - 1, :], ALU.add)


def dense_tiles(k, pe, n0, n_slabs, n_k, x_hi, x_lo, banks, bank_free):
    for s in range(n_slabs):
        group, g = divmod(s, len(n_k))
        m = k.order[n0 + s]
        pe.wait_ge(k.raw_split, m + 1)
        w_hi = k.slab_view(k.w_hi, m % SPL, 0, 256, n_k[g], 256)
        w_lo = k.slab_view(k.w_lo, m % SPL, 0, 256, n_k[g], 256)
        for half in range(2):
            tile = 2 * group + half
            if g == 0:
                bank_free(tile)
            c = slice(half * P, (half + 1) * P)
            for q in range(n_k[g]):
                kt = sum(n_k[:g]) + q
                last = k.three(pe, banks[tile % len(banks)][:, 0:T], w_hi[:, q, c], w_lo[:, q, c], x_hi[:, kt, :],
                               x_lo[:, kt, :], start=(kt == 0), stop=(kt == sum(n_k) - 1))
        last.then_inc(k.split_read, 1)


def conv_phase(k, h_hi, h_lo, qkv, z_silu, last_rows):
    nc, n0, n_slabs = k.nc, k.first["w_in"], 16
    banks = range(6)
    k.start_splits(n0)
    with nc.sbuf_tensor("xp", [P, 4, T + 6], F32) as xp, nc.sbuf_tensor("conv_acc", [P, 2, T + 3], F32) as acc, \
            nc.semaphore("z_ready") as z_ready, \
            nc.semaphore("xp_ready") as xp_ready, nc.semaphore("xp_ctx") as xp_ctx, nc.semaphore("conv_done") as conv_done, \
            nc.semaphore("conv_step") as conv_step, nc.semaphore("silu_done") as silu_done, \
            nc.semaphore("rows_kept") as rows_kept, nc.Block() as block:
        @block.sync
        def _(sp):
            for n in range(n0, n0 + n_slabs):
                k.load(sp, n + RAW)

        @block.tensor
        def _(pe):
            def bank_free(tile):
                if tile - 6 >= QKV_T:
                    pe.wait_ge(z_ready, tile - 5 - QKV_T)
                elif tile >= 6:
                    pe.wait_ge(xp_ready, tile - 5)
            dense_tiles(k, pe, n0, n_slabs, [KT], h_hi, h_lo, k.ps[0:6], bank_free)

        def read_before(s):
            return k.order[n0] + s

        @block.scalar
        def _(act):
            def silu(t):
                act.wait_ge(conv_done, t + 1)
                act.activation(qkv[:, t, 0:TP], acc[:, t % 2, 0:TP], ACT.Silu)
                act.activation(qkv[:, t, TP:T], acc[:, t % 2, TP + 3:T + 3], ACT.Silu).then_inc(silu_done, 1)

            def finish(s):
                act.wait_ge(k.split_read, read_before(s) + 1)
                for t in (2 * s, 2 * s + 1):
                    bank = k.ps[banks[t % 6]]
                    if t < QKV_T:
                        if t >= 4:
                            act.wait_ge(conv_done, t - 3)
                            act.wait_ge(rows_kept, t - 3)
                        act.activation(xp[:, t % 4, 3:3 + TP], bank[:, 0:TP], ACT.Copy)
                        act.activation(xp[:, t % 4, TP + 6:T + 6], bank[:, TP:T], ACT.Copy).then_inc(xp_ready, 1)
                    else:
                        act.activation(z_silu[:, t - QKV_T, :], bank[:, 0:T], ACT.Silu).then_inc(z_ready, 1)

            k.ahead_hi(act, n0 + AHEAD - 1)
            for s in range(n_slabs):
                if s >= 1:
                    finish(s - 1)
                k.ahead_hi(act, n0 + s + AHEAD)
                if s >= 2:
                    for t in (2 * s - 4, 2 * s - 3):
                        if t < QKV_T:
                            silu(t)
            finish(n_slabs - 1)

        @block.vector
        def _(dve):
            def conv(t):
                dve.wait_ge(xp_ready, t + 1)
                dve.wait_ge(xp_ctx, t + 1)
                if t >= 2:
                    dve.wait_ge(silu_done, t - 1)
                w, x, a = k.conv_cols[:, t, :], xp[:, t % 4, :], acc[:, t % 2, :]
                dve.tensor_scalar(a, x[:, 0:T + 3], w[:, 0:1], None, ALU.mult).then_inc(conv_step, 1)
                for tap in range(1, CONV):
                    dve.wait_ge(conv_step, 3 * t + tap)
                    ins = dve.scalar_tensor_tensor(a, x[:, tap:tap + T + 3], w[:, tap:tap + 1], a, ALU.mult, ALU.add)
                    ins.then_inc(conv_step if tap < CONV - 1 else conv_done, 1)

            k.ahead_lo(dve, n0 + AHEAD - 1)
            for s in range(n_slabs):
                k.ahead_lo(dve, n0 + s + AHEAD)
                if s >= 1:
                    for t in (2 * s - 2, 2 * s - 1):
                        if t < QKV_T:
                            conv(t)

        @block.gpsimd
        def _(pool):
            for t in range(QKV_T):
                if t >= 4:
                    pool.wait_ge(conv_done, t - 3)
                pool.memset(xp[:, t % 4, 0:3], 0.0)
                pool.tensor_copy(xp[:, t % 4, TP + 3:TP + 6], k.conv_cols[:, t, 4:7]).then_inc(xp_ctx, 1)
                pool.wait_ge(xp_ready, t + 1)
                pool.tensor_copy(last_rows[:, t, 0:3], xp[:, t % 4, TP:TP + 3])
                pool.tensor_copy(last_rows[:, t, 3:6], xp[:, t % 4, T + 3:T + 6]).then_inc(rows_kept, 1)


def gates_phase(k, h32, beta, g):
    nc = k.nc
    with nc.sbuf_tensor("gate_a", [CHUNK, NCH, H], F32) as ta, nc.sbuf_tensor("gate_l", [CHUNK, NCH, H], F32) as tl, \
            nc.semaphore("ba_done") as ba_done, nc.semaphore("a_ready") as a_ready, \
            nc.semaphore("exp_ready") as exp_ready, nc.Block() as block:
        psum = k.ps[7][0:CHUNK, 0:NCH * 2 * H].rearrange("p (c j) -> p c j", j=2 * H)

        @block.tensor
        def _(pe):
            for c in range(NCH):
                for kt in range(KT):
                    last = pe.matmul(psum[:, c, :], h32[:, kt, c * CHUNK:(c + 1) * CHUNK], k.wba[:, kt, :],
                                     start=(kt == 0), stop=(kt == KT - 1))
            last.then_inc(ba_done, 1)

        @block.vector
        def _(dve):
            run = k.dve_chain.on(dve)
            dve.wait_ge(ba_done, 1)
            run(dve.tensor_copy(beta[:], psum[:, :, 0:H]))
            dve.tensor_tensor(ta[:], psum[:, :, H:2 * H], k.dt_bias[:].unsqueeze(1).to_broadcast([CHUNK, NCH, H]),
                              ALU.add).then_inc(a_ready, 1)
            dve.wait_ge(exp_ready, 1)
            run(dve.tensor_scalar(beta[:], beta[:], 1.0, None, ALU.add))
            run(dve.reciprocal(beta[:], beta[:]))
            run(dve.scalar_tensor_tensor(tl[:], ta[:], 0.0, tl[:], ALU.max, ALU.add))
            run(dve.tensor_tensor(tl[:], tl[:], k.a_log[:].unsqueeze(1).to_broadcast([CHUNK, NCH, H]), ALU.mult))
            dve.tensor_scalar(g[:], tl[:], -1.0, None, ALU.mult)

        @block.scalar
        def _(act):
            run = k.act_chain.on(act)
            act.wait_ge(a_ready, 1)
            run(act.activation(beta[:], beta[:], ACT.Exp, scale=-1.0))
            run(act.activation(k.a_log[:], k.a_log[:], ACT.Exp))
            run(act.activation(tl[:], ta[:], ACT.Abs))
            run(act.activation(tl[:], tl[:], ACT.Exp, scale=-1.0))
            act.activation(tl[:], tl[:], ACT.Ln, bias=1.0).then_inc(exp_ready, 1)


def unit_phase(k, qkv):
    nc, pieces = k.nc, 2 * H * T // 512
    flat = qkv[:, 0:2 * H, :].rearrange("p t n -> p (t n)")
    with nc.sbuf_tensor("unit_sq", [P, 2, 512], F32) as sq, nc.sbuf_tensor("unit_inv", [P, 2, 512], F32) as inv, \
            nc.semaphore("u_squared") as squared, nc.semaphore("u_summed") as summed, \
            nc.semaphore("u_inverse") as inverse, nc.semaphore("u_root") as root, \
            nc.semaphore("u_scaled") as scaled, nc.Block() as block:
        @block.scalar
        def _(act):
            for j in range(pieces + 1):
                if j < pieces:
                    if j >= 2:
                        act.wait_ge(summed, j - 1)
                    act.activation(sq[:, j % 2, :], flat[:, j * 512:(j + 1) * 512], ACT.Square).then_inc(squared, 1)
                if j >= 1:
                    act.wait_ge(inverse, j)
                    act.activation(inv[:, (j - 1) % 2, :], inv[:, (j - 1) % 2, :], ACT.Sqrt).then_inc(root, 1)

        @block.tensor
        def _(pe):
            for j in range(pieces):
                pe.wait_ge(squared, j + 1)
                if j >= 4:
                    pe.wait_ge(inverse, j - 3)
                pe.matmul(k.ps[j % 4][:], k.ones[:], sq[:, j % 2, :], start=True, stop=True).then_inc(summed, 1)

        @block.vector
        def _(dve):
            run = k.dve_chain.on(dve)
            for j in range(pieces + 1):
                if j < pieces:
                    dve.wait_ge(summed, j + 1)
                    if j >= 2:
                        dve.wait_ge(scaled, j - 1)
                    run(dve.tensor_scalar(inv[:, j % 2, :], k.ps[j % 4][:], 1e-6, None, ALU.add))
                    dve.reciprocal(inv[:, j % 2, :], inv[:, j % 2, :]).then_inc(inverse, 1)
                if j >= 1:
                    dve.wait_ge(root, j)
                    x = flat[:, (j - 1) * 512:j * 512]
                    dve.scalar_tensor_tensor(x, x, DK ** -0.5 if j - 1 < pieces // 2 else 1.0, inv[:, (j - 1) % 2, :],
                                             ALU.mult, ALU.mult).then_inc(scaled, 1)


LEVELS = (2, 4, 8, 16, 32)


def block_masks(k, level_mask):
    with k.nc.Block() as block:
        @block.gpsimd
        def _(pool):
            run = k.pool_chain.on(pool)
            for n in range(6):
                b = 1 << n
                m = level_mask[:, n, :].rearrange("p (j r) -> p j r", r=2 * b)
                run(pool.memset(level_mask[:, n, :], 1.0))
                run(pool.affine_select(out=m, in_=m, compare_op=ALU.is_ge, fill=0.0, base=0,
                                       pattern=[[-2 * b, 32 // b], [0, 2 * b]], channel_multiplier=1))
                run(pool.affine_select(out=m, in_=m, compare_op=ALU.is_ge, fill=0.0, base=b - 1,
                                       pattern=[[2 * b, 32 // b], [0, 2 * b]], channel_multiplier=-1))
                run(pool.affine_select(out=m, in_=m, compare_op=ALU.is_ge, fill=0.0, base=-b,
                                       pattern=[[0, 32 // b], [1, 2 * b]], channel_multiplier=0))


def delta_phase(k, qkv, beta, g, oT):
    nc, i, o = k.nc, k.i, k.o
    PE = ["rows", "gram", "turn_v", "turn_k", "turn_y"]
    DVE = ["gates", "diff", "kb", "decayed", "lower", "y0", "vb", "ktail"]
    AC = ["eg", "et", "x0"]
    for n in range(len(LEVELS)):
        PE += [f"p{n}", f"xy{n}"]
        DVE += [f"xy{n}"]
        AC += [f"p{n}"]
    PE += ["ks", "vnew", "out", "state"]
    DVE += ["rhs", "state"]
    AC += ["vnew", "out"]

    def at(steps, c, name):
        return c * len(steps) + steps.index(name) + 1

    n0, n_ada = k.first["ada_rest"], 48
    with ExitStack() as mem:
        def sb(name, shape):
            return mem.enter_context(nc.sbuf_tensor(name, shape, F32))

        def sem(name):
            return mem.enter_context(nc.semaphore(name))
        gc = sb("gc", [CHUNK, NCH, H])
        tail = sb("tail", [CHUNK, H])
        level_mask = sb("level_mask", [CHUNK, 6, CHUNK])
        block_masks(k, level_mask)
        ug, bg = sb("g_rows", [CHUNK, H, CHUNK]), sb("beta_rows", [CHUNK, H, CHUNK])
        eg = sb("exp_gc", [P, H, CHUNK])
        et = sb("decay", [CHUNK, H, CHUNK])
        kb, kbe, qd = (sb(n, [P, H, CHUNK]) for n in ("kb", "kbe", "q_dec"))
        lt, at_qk, x, y = (sb(n, [CHUNK, H, CHUNK]) for n in ("lower_t", "a_qk_t", "inv", "inv_t"))
        pm, lb = ug, bg
        vb, kt_ = sb("v_beta", [CHUNK, H, DK]), sb("k_tail", [CHUNK, H, DK])
        vn = sb("delta_v", [CHUNK, H, DK])
        state = [sb("state_p", [P, H, DK]), sb("state_s", [P, H, DK])]
        pe_step, dve_step, act_step, lb_step = sem("pe_step"), sem("dve_step"), sem("act_step"), sem("lb_step")
        state_in, gc_sum, gc_ready, ada_done = sem("state_in"), sem("gc_sum"), sem("gc_ready"), sem("ada_done")
        block = mem.enter_context(nc.Block())
        b = k.ps

        def heads(bank):
            return bank[:].rearrange("p (h n) -> p h n", h=H)

        def pair(lo_bank, hi_bank, h):
            return (lo_bank, hi_bank)[h // 4][0:CHUNK, (h % 4) * DK:(h % 4 + 1) * DK]

        @block.sync
        def _(sp):
            sp.dma_start(state[1][:], i["state_delta"][0, 0].rearrange("h a e -> a h e")).then_inc(state_in, 16)
            for n in range(n0, n0 + n_ada):
                k.load(sp, n + RAW)
            for s, c in ((0, NCH - 2), (1, NCH - 1)):
                sp.wait_ge(dve_step, at(DVE, c, "state"))
                k.store(sp, 0, o["delta"][s][0, 0].rearrange("h a e -> a h e"), state[s][:])

        @block.tensor
        def _(pe):
            pe.matmul(b[1][0:CHUNK, 0:NCH * H], k.tri_incl[0:CHUNK, 0:CHUNK], g[:].rearrange("p c h -> p (c h)"),
                      start=True, stop=True).then_inc(gc_sum, 1)
            taken = [0]

            def ada():
                if taken[0] < n_ada:
                    ada_slab(k, pe, n0 + taken[0], 4 * taken[0], b[0])
                    taken[0] += 1

            for c in range(NCH):
                q = qkv[:, 0:H, c * CHUNK:(c + 1) * CHUNK]
                key = qkv[:, H:2 * H, c * CHUNK:(c + 1) * CHUNK]
                v = qkv[:, 2 * H:3 * H, c * CHUNK:(c + 1) * CHUNK]
                s = state[c // (NCH - 1)]
                pe.wait_ge(dve_step, at(DVE, c, "gates"))
                pe.wait_ge(gc_ready, 1)
                pe.matmul(b[1][:], k.ones[0:CHUNK, :], ug[:].rearrange("p h n -> p (h n)"), start=True, stop=True)
                pe.matmul(b[2][:], k.ones[0:CHUNK, :], bg[:].rearrange("p h n -> p (h n)"), start=True,
                          stop=True).then_inc(pe_step, 1)
                ada()
                pe.wait_ge(dve_step, at(DVE, c, "kb"))
                for h in range(H):
                    pe.matmul(heads(b[3])[0:CHUNK, h, :], key[:, h, :], kb[:, h, :], start=True, stop=True)
                for h in range(H):
                    last = pe.matmul(heads(b[4])[0:CHUNK, h, :], key[:, h, :], q[:, h, :], start=True, stop=True)
                last.then_inc(pe_step, 1)
                for h in range(H):
                    last = pe.transpose(pair(b[5], b[6], h), v[:, h, :], k.ident[:])
                last.then_inc(pe_step, 1)
                if c >= 1:
                    pe.wait_ge(act_step, at(AC, c - 1, "out"))
                for h in range(H):
                    last = pe.transpose(pair(b[7], b[2], h), key[:, h, :], k.ident[:])
                last.then_inc(pe_step, 1)
                pe.wait_ge(dve_step, at(DVE, c, "y0"))
                for h in range(H):
                    last = pe.transpose(heads(b[3])[0:CHUNK, h, :], y[:, h, :], k.ident[0:CHUNK, 0:CHUNK])
                last.then_inc(pe_step, 1)
                ada()
                pe.wait_ge(dve_step, at(DVE, c, "vb"))
                for n in range(len(LEVELS)):
                    pe.wait_ge(lb_step, len(LEVELS) * c + n + 1)
                    if n == 0:
                        pe.wait_ge(act_step, at(AC, c, "x0"))
                    else:
                        pe.wait_ge(dve_step, at(DVE, c, f"xy{n - 1}"))
                    for h in range(H):
                        last = pe.matmul(heads(b[4])[0:CHUNK, h, :], lb[:, h, :], x[:, h, :], start=True, stop=True)
                    last.then_inc(pe_step, 1)
                    ada()
                    pe.wait_ge(act_step, at(AC, c, f"p{n}"))
                    for h in range(H):
                        pe.matmul(heads(b[5])[0:CHUNK, h, :], y[:, h, :], pm[:, h, :], start=True, stop=True)
                    for h in range(H):
                        last = pe.matmul(heads(b[6])[0:CHUNK, h, :], pm[:, h, :], y[:, h, :], start=True, stop=True)
                    last.then_inc(pe_step, 1)
                    if n % 2 == 0:
                        ada()
                pe.wait_ge(dve_step, at(DVE, c, "decayed"))
                if c == NCH - 1:
                    pe.wait_ge(state_in, 16)
                elif c >= 1:
                    pe.wait_ge(dve_step, at(DVE, c - 1, "state"))
                for h in range(H):
                    last = pe.matmul(pair(b[1], b[2], h), kbe[:, h, :], s[:, h, :], start=True, stop=True)
                last.then_inc(pe_step, 1)
                pe.wait_ge(dve_step, at(DVE, c, "rhs"))
                for h in range(H):
                    last = pe.matmul(pair(b[3], b[4], h), y[:, h, :], vb[:, h, :], start=True, stop=True)
                last.then_inc(pe_step, 1)
                pe.wait_ge(act_step, at(AC, c, "vnew"))
                for h in range(H):
                    pe.matmul(heads(b[7])[:, h, :], s[:, h, :], qd[:, h, :], start=True, stop=False)
                    last = pe.matmul(heads(b[7])[:, h, :], vn[:, h, :], at_qk[:, h, :], start=False, stop=True)
                last.then_inc(pe_step, 1)
                for h in range(H):
                    bank = (b[5], b[6])[h // 4]
                    last = pe.matmul(bank[:, (h % 4) * DK:(h % 4 + 1) * DK], kt_[:, h, :], vn[:, h, :], start=True,
                                     stop=True)
                last.then_inc(pe_step, 1)
            while taken[0] < n_ada:
                ada()

        @block.vector
        def _(dve):
            run = k.dve_chain.on(dve)
            run(dve.memset(state[0][:], 0.0))
            dve.wait_ge(gc_sum, 1)
            dve.tensor_copy(gc[:].rearrange("p c h -> p (c h)"), b[1][0:CHUNK, 0:NCH * H]).then_inc(gc_ready, 1)
            ident = k.ident[0:CHUNK, 0:CHUNK].unsqueeze(1).to_broadcast([CHUNK, H, CHUNK])
            tri = k.tri_incl[0:CHUNK, 0:CHUNK].unsqueeze(1).to_broadcast([CHUNK, H, CHUNK])

            def over(a, n=CHUNK):
                return a.unsqueeze(2).to_broadcast([CHUNK, H, n])

            for c in range(NCH):
                q = qkv[:, 0:H, c * CHUNK:(c + 1) * CHUNK]
                key = qkv[:, H:2 * H, c * CHUNK:(c + 1) * CHUNK]
                s = state[c // (NCH - 1)]
                if c >= 1:
                    dve.wait_ge(pe_step, at(PE, c - 1, "xy4"))
                dve.tensor_tensor(ug[:], tri, over(g[:, c, :]), ALU.mult)
                dve.tensor_tensor(bg[:], ident, over(beta[:, c, :]), ALU.mult).then_inc(dve_step, 1)
                dve.wait_ge(pe_step, at(PE, c, "rows"))
                dve.wait_ge(act_step, at(AC, c, "eg"))
                dve.wait_ge(gc_ready, 1)
                run(dve.tensor_tensor(et[:], heads(b[1])[0:CHUNK], over(gc[:, c, :]), ALU.subtract))
                dve.tensor_tensor(tail[:], heads(b[1])[0:CHUNK, :, CHUNK - 1], gc[:, c, :], ALU.subtract)
                dve.tensor_scalar(et[:], et[:], 0.0, None, ALU.min).then_inc(dve_step, 1)
                dve.tensor_tensor(kb[:], key, heads(b[2]), ALU.mult).then_inc(dve_step, 1)
                dve.wait_ge(dve_step, at(DVE, c, "kb"))
                dve.tensor_tensor(kbe[:], kb[:], eg[:], ALU.mult)
                dve.tensor_tensor(qd[:], q, eg[:], ALU.mult).then_inc(dve_step, 1)
                dve.wait_ge(act_step, at(AC, c, "et"))
                run(dve.tensor_tensor(et[:], et[:], tri, ALU.mult))
                dve.wait_ge(pe_step, at(PE, c, "gram"))
                dve.tensor_tensor(lt[:], heads(b[3])[0:CHUNK], et[:], ALU.mult)
                dve.tensor_tensor(at_qk[:], heads(b[4])[0:CHUNK], et[:], ALU.mult).then_inc(dve_step, 1)
                dve.wait_ge(dve_step, at(DVE, c, "lower"))
                run(dve.tensor_tensor(y[:], lt[:], level_mask[:, 0, :].unsqueeze(1).to_broadcast([CHUNK, H, CHUNK]),
                                      ALU.mult))
                dve.tensor_tensor(y[:], ident, y[:], ALU.subtract).then_inc(dve_step, 1)
                dve.wait_ge(pe_step, at(PE, c, "turn_v"))
                for half in range(2):
                    hs = slice(4 * half, 4 * half + 4)
                    last = dve.tensor_tensor(vb[:, hs, :], b[5 + half][0:CHUNK, :].rearrange("p (h n) -> p h n", h=4),
                                             beta[:, c, hs].unsqueeze(2).to_broadcast([CHUNK, 4, DK]), ALU.mult)
                last.then_inc(dve_step, 1)
                dve.wait_ge(pe_step, at(PE, c, "turn_k"))
                for half in range(2):
                    hs = slice(4 * half, 4 * half + 4)
                    bank = (b[7], b[2])[half]
                    last = dve.tensor_tensor(kt_[:, hs, :], bank[0:CHUNK, :].rearrange("p (h n) -> p h n", h=4),
                                             tail[:, hs].unsqueeze(2).to_broadcast([CHUNK, 4, DK]), ALU.mult)
                last.then_inc(dve_step, 1)
                for n in range(len(LEVELS)):
                    dve.wait_ge(pe_step, at(PE, c, f"xy{n}"))
                    dve.tensor_tensor(x[:], x[:], heads(b[5])[0:CHUNK], ALU.subtract)
                    dve.tensor_tensor(y[:], y[:], heads(b[6])[0:CHUNK], ALU.subtract).then_inc(dve_step, 1)
                    dve.wait_ge(dve_step, at(DVE, c, f"xy{n}"))
                dve.wait_ge(pe_step, at(PE, c, "ks"))
                for half in range(2):
                    hs = slice(4 * half, 4 * half + 4)
                    last = dve.tensor_tensor(vb[:, hs, :], vb[:, hs, :],
                                             b[1 + half][0:CHUNK, :].rearrange("p (h n) -> p h n", h=4), ALU.subtract)
                last.then_inc(dve_step, 1)
                dve.wait_ge(pe_step, at(PE, c, "state"))
                if c == NCH - 1:
                    dve.wait_ge(state_in, 16)
                for h in range(H):
                    last = dve.scalar_tensor_tensor(s[:, h, :], s[:, h, :], eg[:, h, CHUNK - 1:CHUNK],
                                                    b[5 + h // 4][:, (h % 4) * DK:(h % 4 + 1) * DK], ALU.mult, ALU.add)
                last.then_inc(dve_step, 1)
                dve.wait_ge(dve_step, at(DVE, c, "state"))
            dve.wait_ge(k.raw_read, 8 + n_ada)
            dve.tensor_tensor(k.mod[:, 16:112, :], b[0][:, 0:192].rearrange("p (t s) -> p t s", s=2),
                              k.vec_a[:, 16:112].unsqueeze(2).to_broadcast([P, 96, 2]), ALU.add)

        @block.gpsimd
        def _(pool):
            for c in range(NCH):
                pool.wait_ge(dve_step, at(DVE, c, "lower"))
                for n in range(len(LEVELS)):
                    if n:
                        pool.wait_ge(pe_step, at(PE, c, f"p{n - 1}"))
                    pool.tensor_tensor(lb[:], lt[:], level_mask[:, n + 1, :].unsqueeze(1).to_broadcast([CHUNK, H, CHUNK]),
                                       ALU.mult).then_inc(lb_step, 1)

        @block.scalar
        def _(act):
            for c in range(NCH):
                act.wait_ge(pe_step, at(PE, c, "rows"))
                if c:
                    act.wait_ge(dve_step, at(DVE, c - 1, "state"))
                act.activation(eg[:], heads(b[1]), ACT.Exp).then_inc(act_step, 1)
                act.wait_ge(dve_step, at(DVE, c, "diff"))
                act.activation(tail[:], tail[:], ACT.Exp)
                act.activation(et[:], et[:], ACT.Exp).then_inc(act_step, 1)
                act.wait_ge(pe_step, at(PE, c, "turn_y"))
                act.activation(x[:], heads(b[3])[0:CHUNK], ACT.Copy).then_inc(act_step, 1)
                for n in range(len(LEVELS)):
                    act.wait_ge(pe_step, at(PE, c, f"p{n}"))
                    act.activation(pm[:], heads(b[4])[0:CHUNK], ACT.Copy).then_inc(act_step, 1)
                act.wait_ge(pe_step, at(PE, c, "vnew"))
                for half in range(2):
                    last = act.activation(vn[:, 4 * half:4 * half + 4, :],
                                          b[3 + half][0:CHUNK, :].rearrange("p (h n) -> p h n", h=4), ACT.Copy)
                last.then_inc(act_step, 1)
                act.wait_ge(pe_step, at(PE, c, "out"))
                act.activation(oT[:, :, c * CHUNK:(c + 1) * CHUNK], heads(b[7]), ACT.Copy).then_inc(act_step, 1)


def conv_rows_phase(k, last_rows):
    nc, o = k.nc, k.o
    with nc.sbuf_tensor("row_out", [6, QKV_T * P], F32) as row_out, nc.semaphore("rows_turned") as turned, \
            nc.semaphore("rows_out") as copied, nc.Block() as block:
        @block.tensor
        def _(pe):
            for q in range(QKV_T // 4):
                for j in range(4):
                    last = pe.transpose(k.ps[1 + q][0:6, j * P:(j + 1) * P], last_rows[:, 4 * q + j, :], k.ident[:])
                last.then_inc(turned, 1)

        @block.vector
        def _(dve):
            for q in range(QKV_T // 4):
                dve.wait_ge(turned, q + 1)
                dve.tensor_copy(row_out[:, q * 512:(q + 1) * 512], k.ps[1 + q][0:6, :]).then_inc(copied, 1)

        @block.sync
        def _(sp):
            sp.wait_ge(copied, QKV_T // 4)
            for s in range(2):
                k.store(sp, 0, o["conv"][s][0, 0], row_out[3 * s:3 * s + 3, :])
            sp.wait_ge(k.stores[0], k.n_store[0])


def gated_norm_phase(k, oT, z_silu, hi, lo):
    nc, pieces = k.nc, H * T // 512
    flat, zf = oT[:].rearrange("p h n -> p (h n)"), z_silu[:].rearrange("p h n -> p (h n)")
    hf, lf = hi[:].rearrange("p h n -> p (h n)"), lo[:].rearrange("p h n -> p (h n)")
    gain = k.vec_b[:, 72:73]
    with nc.sbuf_tensor("o_sq", [P, 2, 512], F32) as sq, nc.sbuf_tensor("o_inv", [P, 2, 512], F32) as inv, \
            nc.semaphore("o_squared") as squared, nc.semaphore("o_summed") as summed, \
            nc.semaphore("o_inverse") as inverse, nc.semaphore("o_root") as root, nc.semaphore("o_scaled") as scaled, \
            nc.semaphore("o_hi") as hi_done, nc.semaphore("o_lo") as lo_done, nc.Block() as block:
        @block.scalar
        def _(act):
            for j in range(pieces):
                if j >= 2:
                    act.wait_ge(summed, j - 1)
                act.activation(sq[:, j % 2, :], flat[:, j * 512:(j + 1) * 512], ACT.Square).then_inc(squared, 1)
            for j in range(pieces):
                act.wait_ge(inverse, j + 1)
                act.activation(inv[:, j % 2, :], inv[:, j % 2, :], ACT.Sqrt).then_inc(root, 1)
                act.wait_ge(scaled, j + 1)
                act.activation(hf[:, j * 512:(j + 1) * 512], flat[:, j * 512:(j + 1) * 512], ACT.Copy).then_inc(hi_done, 1)

        @block.tensor
        def _(pe):
            for j in range(pieces):
                pe.wait_ge(squared, j + 1)
                pe.matmul(k.ps[1 + j][:], k.ones[:], sq[:, j % 2, :], start=True, stop=True).then_inc(summed, 1)

        @block.vector
        def _(dve):
            run = k.dve_chain.on(dve)
            for j in range(pieces):
                c = slice(j * 512, (j + 1) * 512)
                dve.wait_ge(summed, j + 1)
                run(dve.tensor_scalar(inv[:, j % 2, :], k.ps[1 + j][:], 1.0 / DK, EPS, ALU.mult, ALU.add))
                dve.reciprocal(inv[:, j % 2, :], inv[:, j % 2, :]).then_inc(inverse, 1)
                dve.wait_ge(root, j + 1)
                run(dve.scalar_tensor_tensor(flat[:, c], flat[:, c], gain, inv[:, j % 2, :], ALU.mult, ALU.mult))
                dve.tensor_tensor(flat[:, c], flat[:, c], zf[:, c], ALU.mult).then_inc(scaled, 1)
                dve.wait_ge(hi_done, j + 1)
                dve.tensor_tensor(lf[:, c], flat[:, c], hf[:, c], ALU.subtract).then_inc(lo_done, 1)


def copy_phase(k, n0, n_slabs, n_k, x_hi, x_lo, dst, name, scale=1.0):
    nc = k.nc
    groups = n_slabs // len(n_k)
    with nc.semaphore(f"emptied_{name}") as emptied, nc.Block() as block:
        @block.sync
        def _(sp):
            for n in range(n0, n0 + n_slabs):
                k.load(sp, n + RAW)

        @block.tensor
        def _(pe):
            def bank_free(tile):
                if tile >= 6:
                    pe.wait_ge(emptied, tile - 5)
            dense_tiles(k, pe, n0, n_slabs, n_k, x_hi, x_lo, k.ps[0:6], bank_free)

        @block.scalar
        def _(act):
            def finish(group):
                act.wait_ge(k.split_read, k.order[n0 + (group + 1) * len(n_k) - 1] + 1)
                for t in (2 * group, 2 * group + 1):
                    act.activation(dst[:, t, :], k.ps[t % 6][:, 0:T], ACT.Copy, scale=scale).then_inc(emptied, 1)

            k.ahead_hi(act, n0 + AHEAD - 1)
            for s in range(n_slabs):
                if s >= 1 and s % len(n_k) == 0:
                    finish(s // len(n_k) - 1)
                k.ahead_hi(act, n0 + s + AHEAD)
            finish(groups - 1)

        @block.vector
        def _(dve):
            k.ahead_lo(dve, n0 + n_slabs - 1 + AHEAD)


def split_phase(k, src, hi, lo, name):
    nc = k.nc
    with nc.semaphore(f"hi_{name}") as hi_done, nc.Block() as block:
        @block.scalar
        def _(act):
            for kt in range(KT):
                act.activation(hi[:, kt, :], src[:, kt, :], ACT.Copy).then_inc(hi_done, 1)

        @block.vector
        def _(dve):
            for kt in range(KT):
                dve.wait_ge(hi_done, kt + 1)
                dve.tensor_tensor(lo[:, kt, :], src[:, kt, :], hi[:, kt, :], ALU.subtract)


def ffn_up_phase(k, h_hi, h_lo, a_hi, a_lo):
    nc, n0, n_slabs = k.nc, k.first["ffn_up"], FT
    with nc.sbuf_tensor("gate_silu", [P, 2, T], F32) as gs, nc.sbuf_tensor("ffn_a", [P, 2, T], F32) as a32, \
            nc.semaphore("gate_ready") as gate_ready, nc.semaphore("a_ready") as a_ready, \
            nc.semaphore("a_hi_ready") as hi_ready, nc.semaphore("a_lo_ready") as lo_ready, nc.Block() as block:
        @block.sync
        def _(sp):
            for n in range(n0, n0 + n_slabs):
                k.load(sp, n + RAW)

        @block.tensor
        def _(pe):
            def bank_free(tile):
                if tile >= 6:
                    pe.wait_ge(a_ready, (tile - 6) // 2 + 1)
            dense_tiles(k, pe, n0, n_slabs, [KT], h_hi, h_lo, k.ps[0:6], bank_free)

        @block.scalar
        def _(act):
            def silu(f):
                act.wait_ge(k.split_read, k.order[n0 + f] + 1)
                if f >= 2:
                    act.wait_ge(a_ready, f - 1)
                act.activation(gs[:, f % 2, :], k.ps[2 * f % 6][:, 0:T], ACT.Silu).then_inc(gate_ready, 1)

            def high(f):
                act.wait_ge(a_ready, f + 1)
                act.activation(a_hi[:, f, :], a32[:, f % 2, :], ACT.Copy).then_inc(hi_ready, 1)

            k.ahead_hi(act, n0 + AHEAD - 1)
            for s in range(n_slabs):
                if s >= 1:
                    silu(s - 1)
                k.ahead_hi(act, n0 + s + AHEAD)
                if s >= 1:
                    high(s - 1)
            silu(n_slabs - 1)
            high(n_slabs - 1)

        @block.vector
        def _(dve):
            def product(f):
                dve.wait_ge(gate_ready, f + 1)
                if f >= 2:
                    dve.wait_ge(lo_ready, f - 1)
                dve.tensor_tensor(a32[:, f % 2, :], k.ps[(2 * f + 1) % 6][:, 0:T], gs[:, f % 2, :],
                                  ALU.mult).then_inc(a_ready, 1)

            def low(f):
                dve.wait_ge(hi_ready, f + 1)
                dve.tensor_tensor(a_lo[:, f, :], a32[:, f % 2, :], a_hi[:, f, :], ALU.subtract).then_inc(lo_ready, 1)

            k.ahead_lo(dve, n0 + AHEAD - 1)
            for s in range(n_slabs):
                if s >= 1:
                    product(s - 1)
                k.ahead_lo(dve, n0 + s + AHEAD)
                if s >= 1:
                    low(s - 1)
            product(n_slabs - 1)
            low(n_slabs - 1)


def value_phase(k, h_hi, h_lo, v_new):
    nc, n0, n_slabs = k.nc, k.first["kv_w2"], 4
    with nc.semaphore("v_emptied") as emptied, nc.Block() as block:
        @block.sync
        def _(sp):
            for n in range(n0, n0 + n_slabs):
                k.load(sp, n + RAW)

        @block.tensor
        def _(pe):
            for s in range(n_slabs):
                m = k.order[n0 + s]
                pe.wait_ge(k.raw_split, m + 1)
                if s >= 2:
                    pe.wait_ge(emptied, s - 1)
                w_hi = k.slab_view(k.w_hi, m % SPL, 0, 256, KT, 256)
                w_lo = k.slab_view(k.w_lo, m % SPL, 0, 256, KT, 256)
                for t, (t0, nt) in enumerate(TOKEN_TILES):
                    for kt in range(KT):
                        x_hi, x_lo = h_hi[:, kt, t0:t0 + nt], h_lo[:, kt, t0:t0 + nt]
                        last = k.three(pe, k.ps[3 * (s % 2) + t][0:nt, 0:256], x_hi, x_lo, w_hi[:, kt, :], w_lo[:, kt, :],
                                       start=(kt == 0), stop=(kt == KT - 1))
                last.then_inc(k.split_read, 1)

        @block.scalar
        def _(act):
            def finish(s):
                act.wait_ge(k.split_read, k.order[n0 + s] + 1)
                for t, (t0, nt) in enumerate(TOKEN_TILES):
                    last = act.activation(v_new[0:nt, t, s * 256:(s + 1) * 256], k.ps[3 * (s % 2) + t][0:nt, 0:256], ACT.Copy)
                last.then_inc(emptied, 1)

            k.ahead_hi(act, n0 + AHEAD - 1)
            for s in range(n_slabs):
                if s >= 1:
                    finish(s - 1)
                k.ahead_hi(act, n0 + s + AHEAD)
            finish(n_slabs - 1)

        @block.vector
        def _(dve):
            k.ahead_lo(dve, n0 + n_slabs - 1 + AHEAD)


KEYS_S = PAST + TS


def forget_phase(k, h32, logf, past_logf, f_cols, neg_rows):
    nc = k.nc
    with nc.sbuf_tensor("lf_t", [P, 3, FH], F32) as lt, nc.semaphore("lf_done") as lf_done, \
            nc.semaphore("lf_pre") as pre, nc.semaphore("lf_ln") as ln_ready, nc.semaphore("lf_ready") as ready, \
            nc.semaphore("sums_done") as sums_done, nc.Block() as block:
        ps = k.ps[6][:, 0:3 * FH].rearrange("p (t h) -> p t h", h=FH)
        prompt = [(logf[:, 0, :], P), (logf[:, 1, :], P)]
        sample = [(past_logf[:, t, :], P) for t in range(PAST // P)] + [(logf[0:TS, 2, :], TS)]

        @block.tensor
        def _(pe):
            for t, (t0, nt) in enumerate(TOKEN_TILES):
                for kt in range(KT):
                    last = pe.matmul(ps[0:nt, t, :], h32[:, kt, t0:t0 + nt], k.wlf[:, kt, :], start=(kt == 0),
                                     stop=(kt == KT - 1))
            last.then_inc(lf_done, 1)
            pe.wait_ge(ready, 1)

            def rows(bank, col, tiles, j):
                n = tiles[j][1]
                for q in range(j + 1):
                    src, nk = tiles[q]
                    rhs = k.tri_incl[0:nk, 0:n] if q == j else k.ones[0:nk, 0:n]
                    last = pe.matmul(bank[0:FH, col:col + n], src, rhs, start=(q == 0), stop=(q == j))
                return last

            rows(k.ps[0], 0, prompt, 0)
            rows(k.ps[0], P, prompt, 1)
            for j in range(4):
                rows(k.ps[1], j * P, sample, j)
            rows(k.ps[0], TP, sample, 4)
            for t, (tiles, j) in enumerate(((prompt, 0), (prompt, 1), (sample, 4))):
                n = tiles[j][1]
                for q in range(j + 1):
                    src, nk = tiles[q]
                    lhs = k.tri_incl[0:nk, 0:n] if q == j else k.ones[0:nk, 0:n]
                    last = pe.matmul(k.ps[2][0:n, t * FH:(t + 1) * FH], lhs, src, start=(q == 0), stop=(q == j))
            last.then_inc(sums_done, 1)

        @block.vector
        def _(dve):
            run = k.dve_chain.on(dve)
            run(dve.memset(logf[:], 0.0))
            run(dve.memset(f_cols[:], 0.0))
            dve.wait_ge(lf_done, 1)
            for t, (t0, nt) in enumerate(TOKEN_TILES):
                last = dve.tensor_tensor(logf[0:nt, t, :], ps[0:nt, t, :], k.b_forget[0:nt], ALU.add)
            last.then_inc(pre, 1)
            dve.wait_ge(ln_ready, 1)
            dve.scalar_tensor_tensor(logf[:], logf[:], 0.0, lt[:], ALU.min, ALU.subtract).then_inc(ready, 1)
            dve.wait_ge(sums_done, 1)
            dve.tensor_scalar(neg_rows[:, 0:TP], k.ps[0][0:FH, 0:TP], -1.0, None, ALU.mult)
            dve.tensor_scalar(neg_rows[:, TP + PAST:TP + KEYS_S], k.ps[0][0:FH, TP:TP + TS], -1.0, None, ALU.mult)
            dve.tensor_scalar(neg_rows[:, TP:TP + PAST], k.ps[1][0:FH, 0:PAST], -1.0, None, ALU.mult)
            for t, (t0, nt) in enumerate(TOKEN_TILES):
                dve.tensor_copy(f_cols[0:nt, t, :], k.ps[2][0:nt, t * FH:(t + 1) * FH])

        @block.scalar
        def _(act):
            run = k.act_chain.on(act)
            act.wait_ge(pre, 1)
            run(act.activation(lt[:], logf[:], ACT.Abs))
            run(act.activation(lt[:], lt[:], ACT.Exp, scale=-1.0))
            act.activation(lt[:], lt[:], ACT.Ln, bias=1.0).then_inc(ln_ready, 1)

        @block.sync
        def _(sp):
            sp.wait_ge(ready, 1)
            k.store(sp, 0, k.o["logf"][0][0].rearrange("(t p) h -> p t h", p=P), logf[:, 0:2, :])
            k.store(sp, 0, k.o["logf"][1][0], logf[0:TS, 2, :])


def key_phase(k, k_new, v_new, past_k, k_past_t, k_rows_p, k_rows_s, caches_in):
    nc, o = k.nc, k.o
    turns = []
    for t, (t0, nt) in enumerate(TOKEN_TILES):
        for half in range(2):
            turns.append(([(k_new[:, 4 * half + q, t0:t0 + nt], P) for q in range(4)], P, nt,
                          (k_rows_p[:, t, :] if t < 2 else k_rows_s)[:, half * 512:(half + 1) * 512]))
    for t in range(PAST // P):
        for half in range(2):
            turns.append(([(past_k[:, t, (4 * half + q) * P:(4 * half + q + 1) * P], P) for q in range(4)], P, P,
                          k_past_t[:, 4 * half:4 * half + 4, t * P:(t + 1) * P]))
    with nc.semaphore("k_turned") as turned, nc.semaphore("k_copied") as copied, nc.Block() as block:
        @block.tensor
        def _(pe):
            pe.wait_ge(caches_in, 48)
            for n, (srcs, width, rows, _) in enumerate(turns):
                if n >= 8:
                    pe.wait_ge(copied, n - 7)
                for q, (src, rows_in) in enumerate(srcs):
                    last = pe.transpose(k.ps[n % 8][0:rows, q * width:(q + 1) * width], src, k.ident[0:rows_in, 0:rows_in])
                last.then_inc(turned, 1)

        @block.vector
        def _(dve):
            for n, (srcs, width, rows, dst) in enumerate(turns):
                dve.wait_ge(turned, n + 1)
                src = k.ps[n % 8][0:rows, :]
                if n >= 6:
                    src = src.rearrange("p (q n) -> p q n", q=4)
                dve.tensor_copy(dst, src).then_inc(copied, 1)

        @block.sync
        def _(sp):
            sp.wait_ge(copied, 6)
            for name, prompt, sample in (("k", k_rows_p, k_rows_s[:]), ("v", v_new[:, 0:2, :], v_new[0:TS, 2, :])):
                k.store(sp, 0, o[name][0][0].rearrange("(t p) h d -> p t (h d)", p=P), prompt)
                k.store(sp, 0, o[name][1][0].rearrange("p h d -> p (h d)"), sample)
            sp.wait_ge(k.stores[0], k.n_store[0])


SCORES = 2 * P + P + TS + PAST
C_Q0, C_Q1, C_NEW, C_PAST = 0, P, 3 * P, 3 * P + TS


def attention_phase(k, qT, k_new, k_past, v_new, v_past, f_cols, neg_rows, mask):
    nc = k.nc
    with ExitStack() as mem:
        def sb(name, shape):
            return mem.enter_context(nc.sbuf_tensor(name, shape, F32))

        def sem(name):
            return mem.enter_context(nc.semaphore(name))
        sc = sb("scores", [P, 2, SCORES])
        pt = sb("probs_t", [P, 2, 3 * P + TS + 4 * TS])
        neg_max, total = sb("neg_max", [P, 2, 3]), sb("total", [P, 2, 3])
        scored, shifted, exped, normed = sem("scored"), sem("shifted"), sem("exped"), sem("normed")
        turned, turned_copied, mixed, out_copied = sem("p_turned"), sem("p_copied"), sem("mixed"), sem("out_copied")
        cleared = sem("cleared")
        block = mem.enter_context(nc.Block())
        b = k.ps
        softmaxes = ((P, C_Q0, C_Q1), (P, C_Q1, C_NEW), (TS, C_NEW, SCORES))

        @block.tensor
        def _(pe):
            def score(h):
                rows = slice(FD * (h % 2), FD * (h % 2) + FD)
                t = h // 2
                if h >= 2:
                    pe.wait_ge(shifted, h - 1)
                b_own, b_past = b[h % 2], b[2 + h % 2]
                head = k.ident[0:FH, h:h + 1]

                def block_of(out, q0, nq, keys, neg):
                    pe.matmul(out, qT[rows, t, q0:q0 + nq], keys, start=True, stop=False)
                    return pe.matmul(out, head.to_broadcast([FH, nq]), neg, start=False, stop=True)

                block_of(b_own[:, C_Q0:C_Q1], 0, P, k_new[rows, t, 0:P], neg_rows[:, 0:P])
                block_of(b_own[:, C_Q1:C_NEW], P, P, k_new[rows, t, 0:TP], neg_rows[:, 0:TP])
                block_of(b_own[0:TS, C_NEW:C_PAST], TP, TS, k_new[rows, t, TP:T], neg_rows[:, TP + PAST:TP + KEYS_S])
                block_of(b_past[0:TS, 0:PAST], TP, TS, k_past[rows, t, :], neg_rows[:, TP:TP + PAST]).then_inc(scored, 1)

            def turn(h):
                pe.wait_ge(normed, h + 1)
                if h >= 1:
                    pe.wait_ge(turned_copied, h)
                s = sc[:, h % 2, :]
                for q in range(3):
                    pe.transpose(b[4][:, q * P:(q + 1) * P], s[:, q * P:(q + 1) * P], k.ident[:])
                pe.transpose(b[4][0:TS, 3 * P:3 * P + TS], s[0:TS, C_NEW:C_PAST], k.ident[0:TS, 0:TS])
                for q in range(4):
                    last = pe.transpose(b[5][:, q * TS:(q + 1) * TS], s[0:TS, C_PAST + q * P:C_PAST + (q + 1) * P],
                                        k.ident[0:TS, 0:TS])
                last.then_inc(turned, 1)

            def mix(h):
                pe.wait_ge(turned_copied, h + 1)
                if h >= 4 and h % 2 == 0:
                    pe.wait_ge(out_copied, h // 2 - 1)
                out = b[6 + (h // 2) % 2][FD * (h % 2):FD * (h % 2) + FD, :]
                p, hc = pt[:, h % 2, :], slice(h * FD, (h + 1) * FD)
                pe.matmul(out[:, 0:P], v_new[:, 0, hc], p[:, 0:P], start=True, stop=True)
                pe.matmul(out[:, P:TP], v_new[:, 0, hc], p[:, P:2 * P], start=True, stop=False)
                pe.matmul(out[:, P:TP], v_new[:, 1, hc], p[:, 2 * P:3 * P], start=False, stop=True)
                for q in range(4):
                    c = C_PAST + q * TS
                    pe.matmul(out[:, TP:T], v_past[:, q, hc], p[:, c:c + TS], start=(q == 0), stop=False)
                pe.matmul(out[:, TP:T], v_new[0:TS, 2, hc], p[0:TS, C_NEW:C_PAST], start=False,
                          stop=True).then_inc(mixed, 1)

            pe.wait_ge(cleared, 1)
            score(0)
            for h in range(FH):
                if h + 1 < FH:
                    score(h + 1)
                turn(h)
                mix(h)

        @block.vector
        def _(dve):
            run = k.dve_chain.on(dve)
            dve.memset(total[:], 1.0)
            run(dve.memset(sc[:], 0.0))
            dve.memset(neg_max[:], 0.0).then_inc(cleared, 1)
            dve.wait_ge(cleared, 1)

            def shift(h):
                dve.wait_ge(scored, h + 1)
                if h >= 2:
                    dve.wait_ge(turned, h - 1)
                s, own, past = sc[:, h % 2, :], b[h % 2], b[2 + h % 2]
                f = f_cols[:, :, h:h + 1]
                dve.scalar_tensor_tensor(s[:, C_Q0:C_Q1], own[:, C_Q0:C_Q1], f[:, 0, :], mask[:, P:2 * P], ALU.add, ALU.add)
                dve.scalar_tensor_tensor(s[:, C_Q1:C_NEW], own[:, C_Q1:C_NEW], f[:, 1, :], mask[:], ALU.add, ALU.add)
                dve.scalar_tensor_tensor(s[0:TS, C_NEW:C_PAST], own[0:TS, C_NEW:C_PAST], f[0:TS, 2, :],
                                         mask[0:TS, P:P + TS], ALU.add, ALU.add)
                run(dve.tensor_scalar(s[0:TS, C_PAST:SCORES], past[0:TS, 0:PAST], f[0:TS, 2, :], None, ALU.add))
                for j, (rows, c0, c1) in enumerate(softmaxes):
                    last = dve.tensor_reduce(neg_max[0:rows, h % 2, j:j + 1], s[0:rows, c0:c1], AX.X, ALU.max)
                run(last)
                dve.tensor_scalar(neg_max[:, h % 2, :], neg_max[:, h % 2, :], -1.0, None, ALU.mult).then_inc(shifted, 1)

            def norm(h):
                dve.wait_ge(exped, h + 1)
                run(dve.reciprocal(total[:, h % 2, :], total[:, h % 2, :]))
                for j, (rows, c0, c1) in enumerate(softmaxes):
                    s = sc[0:rows, h % 2, c0:c1]
                    last = dve.tensor_scalar(s, s, total[0:rows, h % 2, j:j + 1], None, ALU.mult)
                last.then_inc(normed, 1)

            shift(0)
            for h in range(FH):
                if h + 1 < FH:
                    shift(h + 1)
                norm(h)

        @block.scalar
        def _(act):
            def exps(h):
                act.wait_ge(shifted, h + 1)
                for j, (rows, c0, c1) in enumerate(softmaxes):
                    s = sc[0:rows, h % 2, c0:c1]
                    last = act.activation(s, s, ACT.Exp, bias=neg_max[0:rows, h % 2, j:j + 1],
                                          accum_out=total[0:rows, h % 2, j:j + 1])
                last.then_inc(exped, 1)

            def copy_out(h):
                act.wait_ge(mixed, h + 1)
                act.activation(qT[:, h // 2, :], b[6 + (h // 2) % 2][:, 0:T], ACT.Copy).then_inc(out_copied, 1)

            exps(0)
            for h in range(FH):
                if h + 1 < FH:
                    exps(h + 1)
                if h >= 2 and h % 2 == 0:
                    copy_out(h - 1)
                act.wait_ge(turned, h + 1)
                if h >= 2:
                    act.wait_ge(mixed, h - 1)
                p = pt[:, h % 2, :]
                act.activation(p[:, 0:3 * P], b[4][:, 0:3 * P], ACT.Copy)
                act.activation(p[0:TS, C_NEW:C_PAST], b[4][0:TS, 3 * P:3 * P + TS], ACT.Copy)
                act.activation(p[:, C_PAST:C_PAST + 4 * TS], b[5][:, 0:4 * TS], ACT.Copy).then_inc(turned_copied, 1)
            copy_out(FH - 1)


def causal_mask(k, mask):
    with k.nc.Block() as block:
        @block.gpsimd
        def _(pool):
            run = k.pool_chain.on(pool)
            run(pool.memset(mask[:], 0.0))
            pool.affine_select(out=mask[:, P:2 * P], in_=mask[:, P:2 * P], compare_op=ALU.is_ge, fill=MASKED, base=0,
                               pattern=[[-1, P]], channel_multiplier=1)


ROUNDS = (T + P - 1) // P
BODIES = ROUNDS * NE // 2


def router_phase(k, h32, h_tok, slot_of, gate_of, bodies):
    nc = k.nc
    with ExitStack() as mem:
        def sb(name, shape, dt=F32):
            return mem.enter_context(nc.sbuf_tensor(name, shape, dt))

        def sem(name):
            return mem.enter_context(nc.semaphore(name))
        logits, best, where, where_f = sb("logits", [P, 3, NE]), sb("best", [P, 3, 8]), sb("where", [P, 3, 8], U32), \
            sb("where_f", [P, 3, 8])
        picked, one, two, gate = (sb(n, [P, 3, NE]) for n in ("picked", "one", "two", "gate"))
        w, slot, most, iota8 = sb("w", [P, 3, 2]), sb("slot", [P, 3, NE]), sb("most", [1, 4]), sb("iota8", [P, NE])
        logits_done, shift, exp_ready, picked_ready, ranked = (sem(n) for n in (
            "logits_done", "top_shift", "top_exp", "picked_ready", "ranked"))
        iota_ready, tok_turned, tok_copied = sem("iota_ready"), sem("tok_turned"), sem("tok_copied")
        block = mem.enter_context(nc.Block())
        lp = k.ps[6][:, 0:3 * NE].rearrange("p (t e) -> p t e", e=NE)
        rp = k.ps[7][:, 0:4 * NE].rearrange("p (t e) -> p t e", e=NE)

        @block.gpsimd
        def _(pool):
            pool.iota(iota8[:], pattern=[[1, NE]], base=0, channel_multiplier=0, allow_small_or_imprecise_dtypes=True)
            pool.iota(k.iota[:], pattern=[[1, P]], base=0, channel_multiplier=0,
                      allow_small_or_imprecise_dtypes=True).then_inc(iota_ready, 1)

        @block.tensor
        def _(pe):
            for t, (t0, nt) in enumerate(TOKEN_TILES):
                for kt in range(KT):
                    last = pe.matmul(lp[0:nt, t, :], h32[:, kt, t0:t0 + nt], k.w_router[:, kt, :], start=(kt == 0),
                                     stop=(kt == KT - 1))
            last.then_inc(logits_done, 1)
            for n in range(6):
                t, half = divmod(n, 2)
                t0, nt = TOKEN_TILES[t]
                for q in range(4):
                    last = pe.transpose(k.ps[n][0:nt, q * P:(q + 1) * P], h32[:, 4 * half + q, t0:t0 + nt], k.ident[:])
                last.then_inc(tok_turned, 1)
            pe.wait_ge(picked_ready, 1)
            for t, (t0, nt) in enumerate(TOKEN_TILES):
                for u in range(t + 1):
                    nu = TOKEN_TILES[u][1]
                    lhs = k.tri_strict[0:nu, 0:nt] if u == t else k.ones[0:nu, 0:nt]
                    pe.matmul(rp[0:nt, t, :], lhs, picked[0:nu, u, :], start=(u == 0), stop=(u == t))
            for u in range(3):
                nu = TOKEN_TILES[u][1]
                last = pe.matmul(rp[0:1, 3, :], k.ones[0:nu, 0:1], picked[0:nu, u, :], start=(u == 0), stop=(u == 2))
            last.then_inc(ranked, 1)

        @block.scalar
        def _(act):
            for n in range(6):
                t, half = divmod(n, 2)
                nt = TOKEN_TILES[t][1]
                act.wait_ge(tok_turned, n + 1)
                act.activation(h_tok[0:nt, t, half * 512:(half + 1) * 512], k.ps[n][0:nt, :], ACT.Copy)
            act.wait_ge(shift, 1)
            act.activation(w[:, :, 1:2], w[:, :, 1:2], ACT.Exp).then_inc(exp_ready, 1)

        @block.vector
        def _(dve):
            run = k.dve_chain.on(dve)
            run(dve.memset(logits[:], 0.0))
            run(dve.memset(slot_of[:], -1.0))
            run(dve.memset(gate_of[:], 0.0))
            run(dve.memset(slot[:], -1.0))
            dve.wait_ge(iota_ready, 1)
            dve.wait_ge(logits_done, 1)
            for t, (t0, nt) in enumerate(TOKEN_TILES):
                run(dve.tensor_tensor(logits[0:nt, t, :], lp[0:nt, t, :], k.b_router[0:nt], ALU.add))
            for t in range(3):
                run(dve.max(best[:, t, :], logits[:, t, :]))
                run(dve.max_index(where[:, t, :], best[:, t, :], logits[:, t, :]))
            run(dve.tensor_copy(where_f[:], where[:]))
            dve.tensor_tensor(w[:, :, 1:2], best[:, :, 1:2], best[:, :, 0:1], ALU.subtract).then_inc(shift, 1)
            for t in range(3):
                dve.tensor_scalar(one[:, t, :], iota8[:], where_f[:, t, 0:1], None, ALU.is_equal)
                run(dve.tensor_scalar(two[:, t, :], iota8[:], where_f[:, t, 1:2], None, ALU.is_equal))
            dve.tensor_tensor(picked[:], one[:], two[:], ALU.add).then_inc(picked_ready, 1)
            dve.wait_ge(exp_ready, 1)
            run(dve.tensor_scalar(w[:, :, 0:1], w[:, :, 1:2], 1.0, None, ALU.add))
            run(dve.reciprocal(w[:, :, 0:1], w[:, :, 0:1]))
            run(dve.tensor_tensor(w[:, :, 1:2], w[:, :, 1:2], w[:, :, 0:1], ALU.mult))
            for t in range(3):
                run(dve.tensor_scalar(gate[:, t, :], one[:, t, :], w[:, t, 0:1], None, ALU.mult))
                run(dve.scalar_tensor_tensor(gate[:, t, :], two[:, t, :], w[:, t, 1:2], gate[:, t, :], ALU.mult, ALU.add))
            dve.wait_ge(ranked, 1)
            for t, (t0, nt) in enumerate(TOKEN_TILES):
                run(dve.scalar_tensor_tensor(slot[0:nt, t, :], rp[0:nt, t, :], 1.0, picked[0:nt, t, :], ALU.add, ALU.mult))
                run(dve.tensor_scalar(slot[0:nt, t, :], slot[0:nt, t, :], -1.0, None, ALU.add))
            for t, (t0, nt) in enumerate(TOKEN_TILES):
                for r in range(ROUNDS):
                    c = slice(NE * r, NE * (r + 1))
                    run(dve.tensor_scalar(slot_of[0:nt, t, c], slot[0:nt, t, :], float(-P * r), None, ALU.add))
                    run(dve.tensor_copy(gate_of[0:nt, t, c], gate[0:nt, t, :]))
            run(dve.tensor_reduce(most[:, 0:1], rp[0:1, 3, :], AX.X, ALU.max))
            run(dve.tensor_scalar(most[:, 1:2], most[:, 0:1], float(P), float(NE // 2), ALU.is_gt, ALU.mult))
            run(dve.tensor_scalar(most[:, 2:3], most[:, 0:1], float(2 * P), float(NE // 2), ALU.is_gt, ALU.mult))
            run(dve.tensor_tensor(most[:, 1:2], most[:, 1:2], most[:, 2:3], ALU.add))
            run(dve.tensor_scalar(bodies[:], most[:, 1:2], float(NE // 2), None, ALU.add))


def expert_phase(k, h_tok, slot_of, gate_of, bodies):
    nc, i = k.nc, k.i
    n0, m0, body = k.first["moe"], k.order[k.first["moe"]], 2 * EXPERT_SLABS
    CH = FF // 256

    def parts_of(g):
        return 2 if g % EXPERT_SLABS < UP_SLABS else 1

    def full_count(w, g):
        slot = (n0 + g) % RAW
        before = k.full_count(n0 - RAW + (slot - n0) % RAW)
        per_body = 16 * sum(parts_of(q) for q in range(body) if (n0 + q) % RAW == slot)
        here = 16 * sum(parts_of(q) for q in range(g % body + 1) if (n0 + q) % RAW == slot)
        return (w + g // body) * per_body + (before + here)

    with ExitStack() as mem:
        def sb(name, shape, dt=F32):
            return mem.enter_context(nc.sbuf_tensor(name, shape, dt))

        def sem(name):
            return mem.enter_context(nc.semaphore(name))
        hg_hi, hg_lo = sb("hg_hi", [P, KT, P], F32R), sb("hg_lo", [P, KT, P], F32R)
        a_hi, a_lo = sb("act_hi", [P, FT, P], F32R), sb("act_lo", [P, FT, P], F32R)
        gs, a32 = sb("e_silu", [P, 2, 256]), sb("e_act", [P, 2, 256])
        o_hi, o_lo = sb("out_hi", [P, D], F32R), sb("out_lo", [P, D], F32R)
        pick = sb("pick", [P, 3, P])
        put = sb("put", [P, 2, T], F32R)
        gate_col, slot_gate = sb("gate_col", [P, 3]), sb("slot_gate", [P, 2])
        silu_done, a_done, turned, a_hi_done, a_lo_done = (sem(n) for n in ("e_silu_done", "e_act_done", "e_turned", "e_hi", "e_lo"))
        pick_ready, gathered, put_turned, hg_hi_done, hg_lo_done, put_copied, gate_copied = (sem(n) for n in (
            "pick_ready", "gathered", "put_turned", "hg_hi_done", "hg_lo_done", "put_copied", "gate_copied"))
        o_hi_done, o_lo_done, scattered, added = (sem(n) for n in ("o_hi_done", "o_lo_done", "scattered", "added"))
        block = mem.enter_context(nc.Block())
        G, TB, DB, Y = k.ps[0:2], k.ps[2:4], k.ps[4:6], k.ps[6:8]

        def build_pick(dve, it):
            for t, (t0, nt) in enumerate(TOKEN_TILES):
                col = slot_of[0:nt, t, bass.ds(it, 1)]
                dve.tensor_scalar(pick[0:nt, t, :], k.iota[0:nt], col, None, ALU.is_equal)
            dve.tensor_copy(gate_col[:], gate_of[:, :, bass.ds(it, 1)].rearrange("p t o -> p (t o)")).then_inc(pick_ready, 1)

        def gather(pe, it):
            pe.wait_ge(pick_ready, it + 1)
            pe.wait_ge(added, it * 8 + 8 if isinstance(it, int) else (it - 1) * 8 + 8)
            for kt in range(KT):
                for t, (t0, nt) in enumerate(TOKEN_TILES):
                    last = pe.matmul(Y[kt // 4][:, (kt % 4) * P:(kt % 4 + 1) * P], h_tok[0:nt, t, kt * P:(kt + 1) * P],
                                     pick[0:nt, t, :], start=(t == 0), stop=(t == 2))
            last.then_inc(gathered, 1)
            for t, (t0, nt) in enumerate(TOKEN_TILES):
                pe.transpose(TB[0][:, t0:t0 + nt], pick[0:nt, t, :], k.ident[0:nt, 0:nt])
            for t, (t0, nt) in enumerate(TOKEN_TILES):
                last = pe.matmul(TB[1][:, 0:1], pick[0:nt, t, :], gate_col[0:nt, t:t + 1], start=(t == 0), stop=(t == 2))
            last.then_inc(put_turned, 1)

        def prepare_act(act, it, par):
            act.wait_ge(gathered, it + 1)
            for half in range(2):
                last = act.activation(hg_hi[:, 4 * half:4 * half + 4, :], Y[half][:].rearrange("p (k n) -> p k n", k=4),
                                      ACT.Copy)
            last.then_inc(hg_hi_done, 1)
            act.wait_ge(put_turned, it + 1)
            act.activation(put[:, par, :], TB[0][:, 0:T], ACT.Copy).then_inc(put_copied, 1)

        def prepare_dve(dve, it, par):
            dve.wait_ge(hg_hi_done, it + 1)
            for half in range(2):
                q = slice(4 * half, 4 * half + 4)
                last = dve.tensor_tensor(hg_lo[:, q, :], Y[half][:].rearrange("p (k n) -> p k n", k=4), hg_hi[:, q, :],
                                         ALU.subtract)
            last.then_inc(hg_lo_done, 1)
            dve.wait_ge(put_turned, it + 1)
            dve.tensor_copy(slot_gate[:, par:par + 1], TB[1][:, 0:1]).then_inc(gate_copied, 1)

        def each_body(eng, run_body):
            n_bodies = eng.value_load(bodies[0:1, 0:1], min_val=NE // 2, max_val=BODIES)
            with eng.Fori(0, BODIES) as w:
                with eng.If(w < n_bodies):
                    run_body(w)
            return n_bodies

        @block.sync
        def _(sp):
            def run_body(w):
                for g in range(body):
                    sp.wait_ge(k.raw_split, w * body + (m0 + g + 1))
                    e, j = divmod(g + RAW, EXPERT_SLABS)
                    expert = (w % 4) * 2 + e if e < 2 else ((w + 1) % 4) * 2
                    slot = (n0 + g) % RAW
                    for words, cols, kts, src in moe_parts(i, expert, j):
                        width = 512 if j < UP_SLABS else D
                        sp.dma_start(k.slab_view(k.raw, slot, words, cols, kts, width), src).then_inc(k.raw_full[slot], 16)
            each_body(sp, run_body)

        @block.tensor
        def _(pe):
            gather(pe, 0)

            def run_body(w):
                for half in range(2):
                    it = w * 2 + half

                    def slab(j):
                        m = m0 + half * EXPERT_SLABS + j
                        pe.wait_ge(k.raw_split, w * body + (m + 1))
                        width, nk = (512, 4) if j < UP_SLABS else (D, 2)
                        return k.slab_view(k.w_hi, m % SPL, 0, width, nk, width), k.slab_view(k.w_lo, m % SPL, 0, width, nk, width)

                    def turn(ch):
                        pe.wait_ge(a_done, it * CH + (ch + 1))
                        if ch < 2:
                            pe.wait_ge((put_copied, gate_copied)[ch], it + 1)
                        else:
                            pe.wait_ge(a_lo_done, it * CH + (ch - 1))
                        for q in range(2):
                            last = pe.transpose(TB[ch % 2][:, q * P:(q + 1) * P], a32[:, ch % 2, q * P:(q + 1) * P], k.ident[:])
                        last.then_inc(turned, 1)

                    pe.wait_ge(hg_lo_done, it + 1)
                    for ch in range(CH):
                        if ch >= 2:
                            pe.wait_ge(a_done, it * CH + (ch - 1))
                        for j in (2 * ch, 2 * ch + 1):
                            w_hi, w_lo = slab(j)
                            for q in range(4):
                                kt = 4 * (j % 2) + q
                                last = k.three(pe, G[ch % 2][:], hg_hi[:, kt, :], hg_lo[:, kt, :], w_hi[:, q, :], w_lo[:, q, :],
                                               start=(kt == 0), stop=(kt == KT - 1))
                            last.then_inc(k.split_read, 1)
                        if ch >= 1:
                            turn(ch - 1)
                    for d in range(DOWN_SLABS):
                        pe.wait_ge(a_lo_done, it * CH + (d + 1))
                        w_hi, w_lo = slab(UP_SLABS + d)
                        for q in range(2):
                            f = 2 * d + q
                            for n in range(2):
                                c = slice(512 * n, 512 * n + 512)
                                last = k.three(pe, DB[n][:], a_hi[:, f, :], a_lo[:, f, :], w_hi[:, q, c], w_lo[:, q, c],
                                               start=(f == 0), stop=(f == FT - 1))
                        last.then_inc(k.split_read, 1)
                        if d == 1:
                            turn(CH - 1)
                    gather(pe, it + 1)
                    pe.wait_ge(o_lo_done, it + 1)
                    pe.wait_ge(hg_lo_done, it + 2)
                    pe.wait_ge(put_copied, it + 1)
                    for f in range(KT):
                        if f >= 2:
                            pe.wait_ge(added, it * 8 + (8 + f - 1))
                        c = slice(f * P, (f + 1) * P)
                        pe.matmul(Y[f % 2][:, 0:T], o_hi[:, c], put[:, half, :], start=True, stop=False)
                        pe.matmul(Y[f % 2][:, 0:T], o_lo[:, c], put[:, half, :], start=False, stop=True).then_inc(scattered, 1)
            n_bodies = each_body(pe, run_body)
            for g in range(RAW):
                pe.wait_ge(k.raw_full[(n0 + g) % RAW], full_count(n_bodies, g))

        def per_slab(split, work, w):
            for g in range(body):
                if g:
                    work(w, g - 1)
                split(w, g + AHEAD)
            work(w, body - 1)

        @block.scalar
        def _(act):
            k.ahead_hi(act, n0 + AHEAD - 1)
            prepare_act(act, 0, 0)

            def split(w, g):
                m, words = m0 + g, SLAB
                act.wait_ge(k.raw_full[(n0 + g) % RAW], full_count(w, g))
                act.wait_ge(k.split_read, w * body + (m - SPL + 1))
                act.activation(k.w_hi[:, m % SPL, :], k.raw[:, (n0 + g) % RAW, :], ACT.Copy).then_inc(k.hi_ready, 1)

            def high(it, ch):
                act.wait_ge(turned, it * CH + (ch + 1))
                act.activation(a_hi[:, 2 * ch:2 * ch + 2, :], TB[ch % 2][:, 0:256].rearrange("p (q n) -> p q n", q=2),
                               ACT.Copy).then_inc(a_hi_done, 1)

            def work(w, g):
                half, j = divmod(g, EXPERT_SLABS)
                it = w * 2 + half
                if j < UP_SLABS and j % 2 == 1:
                    ch = j // 2
                    act.wait_ge(k.split_read, w * body + (m0 + g + 1))
                    if ch >= 2:
                        act.wait_ge(a_done, it * CH + (ch - 1))
                    act.activation(gs[:, ch % 2, :], G[ch % 2][:, 0:256], ACT.Silu).then_inc(silu_done, 1)
                    if ch >= 1:
                        high(it, ch - 1)
                elif j == UP_SLABS + 1:
                    high(it, CH - 1)
                elif j == EXPERT_SLABS - 1:
                    act.wait_ge(k.split_read, w * body + (m0 + g + 1))
                    act.wait_ge(gate_copied, it + 1)
                    for n in range(2):
                        last = act.activation(o_hi[:, n * 512:(n + 1) * 512], DB[n][:], ACT.Copy,
                                              scale=slot_gate[:, half:half + 1])
                    last.then_inc(o_hi_done, 1)
                    prepare_act(act, it + 1, 1 - half)
            each_body(act, lambda w: per_slab(split, work, w))

        @block.vector
        def _(dve):
            for kt in range(KT):
                dve.memset(k.yT[:, kt, :], 0.0).then_inc(added, 1)
            build_pick(dve, 0)
            k.ahead_lo(dve, n0 + AHEAD - 1)
            prepare_dve(dve, 0, 0)

            def split(w, g):
                m = m0 + g
                dve.wait_ge(k.raw_full[(n0 + g) % RAW], full_count(w, g))
                dve.wait_ge(k.hi_ready, w * body + (m + 1))
                dve.tensor_tensor(k.w_lo[:, m % SPL, :], k.raw[:, (n0 + g) % RAW, :], k.w_hi[:, m % SPL, :],
                                  ALU.subtract).then_inc(k.raw_split, 1)

            def low(it, ch):
                q = slice(2 * ch, 2 * ch + 2)
                dve.wait_ge(a_hi_done, it * CH + (ch + 1))
                dve.tensor_tensor(a_lo[:, q, :], TB[ch % 2][:, 0:256].rearrange("p (q n) -> p q n", q=2), a_hi[:, q, :],
                                  ALU.subtract).then_inc(a_lo_done, 1)

            def work(w, g):
                half, j = divmod(g, EXPERT_SLABS)
                it = w * 2 + half
                if j < UP_SLABS and j % 2 == 1:
                    ch = j // 2
                    dve.wait_ge(silu_done, it * CH + (ch + 1))
                    if ch >= 2:
                        dve.wait_ge(turned, it * CH + (ch - 1))
                    dve.tensor_tensor(a32[:, ch % 2, :], G[ch % 2][:, 256:512], gs[:, ch % 2, :], ALU.mult).then_inc(a_done, 1)
                    if ch >= 1:
                        low(it, ch - 1)
                elif j == UP_SLABS + 1:
                    low(it, CH - 1)
                elif j == 10:
                    dve.wait_ge(put_turned, it + 1)
                    build_pick(dve, it + 1)
                elif j == EXPERT_SLABS - 1:
                    dve.wait_ge(o_hi_done, it + 1)
                    for n in range(2):
                        c = slice(n * 512, (n + 1) * 512)
                        last = dve.scalar_tensor_tensor(o_lo[:, c], DB[n][:], slot_gate[:, half:half + 1], o_hi[:, c],
                                                        ALU.mult, ALU.subtract)
                    last.then_inc(o_lo_done, 1)
                    prepare_dve(dve, it + 1, 1 - half)
                    for f in range(KT):
                        dve.wait_ge(scattered, it * 8 + (f + 1))
                        dve.tensor_tensor(k.yT[:, f, :], k.yT[:, f, :], Y[f % 2][:, 0:T], ALU.add).then_inc(added, 1)
            each_body(dve, lambda w: per_slab(split, work, w))


def output_phase(k):
    nc = k.nc
    with nc.sbuf_tensor("y_rows", [P, 3, D], F32) as rows, nc.semaphore("y_turned") as turned, \
            nc.semaphore("y_copied") as copied, nc.Block() as block:
        @block.tensor
        def _(pe):
            for n in range(6):
                t, half = divmod(n, 2)
                t0, nt = TOKEN_TILES[t]
                for q in range(4):
                    last = pe.transpose(k.ps[n][0:nt, q * P:(q + 1) * P], k.xT[:, 4 * half + q, t0:t0 + nt], k.ident[:])
                last.then_inc(turned, 1)

        @block.vector
        def _(dve):
            for n in range(6):
                t, half = divmod(n, 2)
                nt = TOKEN_TILES[t][1]
                dve.wait_ge(turned, n + 1)
                dve.tensor_copy(rows[0:nt, t, half * 512:(half + 1) * 512], k.ps[n][0:nt, :]).then_inc(copied, 1)

        @block.sync
        def _(sp):
            for t in range(2):
                sp.wait_ge(copied, 2 * t + 2)
                k.store(sp, 0, k.o["y"][0][0, t * P:(t + 1) * P, :], rows[:, t, :])
            sp.wait_ge(copied, 6)
            k.store(sp, 0, k.o["y"][1][0], rows[0:TS, 2, :])
            sp.wait_ge(k.stores[0], k.n_store[0])


def build(nc, i, o):
    ctx = ExitStack()
    with ctx:
        k = Kernel(nc, ctx, i, o)
        setup_phase(k)
        ada_phase(k)

        def parts(stack, name, tiles=KT):
            return tuple(stack.enter_context(nc.sbuf_tensor(f"{name}_{part}", [P, tiles, T], F32R)) for part in ("hi", "lo"))

        with ExitStack() as gdn:
            def sb(name, shape, dt=F32):
                return gdn.enter_context(nc.sbuf_tensor(name, shape, dt))
            z_silu = sb("z_silu", [P, H, T])
            with nc.sbuf_tensor("qkv", [P, QKV_T, T], F32) as qkv, \
                    nc.sbuf_tensor("last_rows", [P, QKV_T, 6], F32) as last_rows, \
                    nc.sbuf_tensor("beta", [CHUNK, NCH, H], F32) as beta, nc.sbuf_tensor("g", [CHUNK, NCH, H], F32) as g:
                with ExitStack() as s:
                    h32 = k.yT
                    h_hi, h_lo = parts(s, "h_mix0")
                    norm_phase(k, k.xT, k.gain("pre_mix", 0), k.mod_tiles(0, SC_M), k.mod_tiles(0, SH_M), h_hi, h_lo,
                               h32, "_m0")
                    conv_phase(k, h_hi, h_lo, qkv, z_silu, last_rows)
                    gates_phase(k, h32, beta, g)
                unit_phase(k, qkv)
                delta_phase(k, qkv, beta, g, k.yT)
                conv_rows_phase(k, last_rows)
            k.start_splits(k.first["w_out"])
            o_hi, o_lo = parts(gdn, "o")
            gated_norm_phase(k, k.yT, z_silu, o_hi, o_lo)
            copy_phase(k, k.first["w_out"], 4, [KT], o_hi, o_lo, k.yT, "w_out")
        residual_phase(k, k.mod_tiles(0, GT_M), k.gain("post_mix", 0), "_m0")

        with ExitStack() as s:
            a_hi, a_lo = parts(s, "ffn_act", FT)
            with ExitStack() as s2:
                h_hi, h_lo = parts(s2, "h_ffn0")
                norm_phase(k, k.xT, k.gain("pre_ffn", 0), k.mod_tiles(0, SC_F), k.mod_tiles(0, SH_F), h_hi, h_lo, None, "_f0")
                ffn_up_phase(k, h_hi, h_lo, a_hi, a_lo)
            copy_phase(k, k.first["ffn_down"], 12, [8, 8, 6], a_hi, a_lo, k.yT, "ffn_down")
        residual_phase(k, k.mod_tiles(0, GT_F), k.gain("post_ffn", 0), "_f0")

        with ExitStack() as s:
            def sb(name, shape, dt=F32):
                return s.enter_context(nc.sbuf_tensor(name, shape, dt))
            k_new, v_new, v_past = sb("k_new", [P, KT, T]), sb("v_new", [P, 3, D]), sb("v_past", [P, PAST // P, D])
            f_cols, neg_rows = sb("f_cols", [P, 3, FH]), sb("neg_rows", [FH, TP + KEYS_S])
            mask = sb("mask", [P, 2 * P])
            past_logf, logf = sb("past_logf", [P, PAST // P, FH]), sb("logf", [P, 3, FH])
            caches_in = s.enter_context(nc.semaphore("caches_in"))
            with nc.Block() as block:
                @block.scalar
                def _(act):
                    act.dma_start(v_past[:], i["cache_v"][0].rearrange("(t p) h d -> p t (h d)", p=P)).then_inc(caches_in, 16)
                    act.dma_start(past_logf[:], i["cache_logf"][0].rearrange("(t p) h -> p t h", p=P)).then_inc(caches_in, 16)
            causal_mask(k, mask)
            kv_scale, kv_shift = k.mod[:, KV_MOD + KT:KV_MOD + 2 * KT, :], k.mod[:, KV_MOD:KV_MOD + KT, :]
            with ExitStack() as s2:
                h_hi, h_lo = parts(s2, "h_kv")
                norm_phase(k, k.xT, k.gain("kv"), kv_scale, kv_shift, h_hi, h_lo, k.yT, "_kv")
                with nc.Block() as block:
                    @block.tensor
                    def _(pe):
                        pe.wait_ge(caches_in, 32)
                forget_phase(k, k.yT, logf, past_logf, f_cols, neg_rows)
                copy_phase(k, k.first["kv_w"], 4, [KT], h_hi, h_lo, k_new, "w_k")
                value_phase(k, h_hi, h_lo, v_new)
            k_past = sb("k_past_t", [P, KT, PAST])
            k_rows_p = k.yT[:].rearrange("p a n -> p (a n)")[:, 0:2 * D].rearrange("p (t n) -> p t n", t=2)
            with nc.sbuf_tensor("past_k", [P, PAST // P, D], F32) as past_k, nc.sbuf_tensor("k_rows_s", [TS, D], F32) as k_rows_s:
                with nc.Block() as block:
                    @block.scalar
                    def _(act):
                        act.dma_start(past_k[:], i["cache_k"][0].rearrange("(t p) h d -> p t (h d)", p=P)).then_inc(caches_in, 16)
                key_phase(k, k_new, v_new, past_k, k_past, k_rows_p, k_rows_s, caches_in)
            with ExitStack() as s2:
                h_hi, h_lo = parts(s2, "h_mix1")
                norm_phase(k, k.xT, k.gain("pre_mix", 1), k.mod_tiles(1, SC_M), k.mod_tiles(1, SH_M), h_hi, h_lo, None, "_m1")
                copy_phase(k, k.first["w_q"], 4, [KT], h_hi, h_lo, k.yT, "w_q", scale=FD ** -0.5)
            attention_phase(k, k.yT, k_new, k_past, v_new, v_past, f_cols, neg_rows, mask)
        with ExitStack() as s:
            o_hi, o_lo = parts(s, "attn_o")
            split_phase(k, k.yT, o_hi, o_lo, "attn_o")
            copy_phase(k, k.first["w_o"], 4, [KT], o_hi, o_lo, k.yT, "w_o")
        residual_phase(k, k.mod_tiles(1, GT_M), k.gain("post_mix", 1), "_m1")

        with ExitStack() as s:
            def sb(name, shape, dt=F32):
                return s.enter_context(nc.sbuf_tensor(name, shape, dt))
            k.iota = sb("iota", [P, P])
            h_tok = sb("h_tok", [P, 3, D])
            slot_of, gate_of = sb("slot_of", [P, 3, ROUNDS * NE + 1]), sb("gate_of", [P, 3, ROUNDS * NE + 1])
            bodies = sb("bodies", [1, 1], I32)
            with ExitStack() as s2:
                h32 = k.yT
                h_hi, h_lo = parts(s2, "h_ffn1")
                norm_phase(k, k.xT, k.gain("pre_ffn", 1), k.mod_tiles(1, SC_F), k.mod_tiles(1, SH_F), h_hi, h_lo, h32, "_f1")
                router_phase(k, h32, h_tok, slot_of, gate_of, bodies)
            expert_phase(k, h_tok, slot_of, gate_of, bodies)
        residual_phase(k, k.mod_tiles(1, GT_F), k.gain("post_ffn", 1), "_f1")
        output_phase(k)


def kernel(**inputs):
    import concourse.bacc as bacc
    from concourse.bass_utils import run_bass_kernel_spmd

    nc = bacc.Bacc("TRN2", target_bir_lowering=False, num_devices=1)
    arrays = {name: np.ascontiguousarray(a) for name, a in inputs.items()}
    build(nc, hbm_inputs(nc, arrays), hbm_outputs(nc))
    got = run_bass_kernel_spmd(nc, [{f"in_{name}": a for name, a in arrays.items()}], core_ids=[0]).results[0]
    order = [("y", 0), ("y", 1)] + [(name, s) for s in range(2) for name in ("k", "v", "logf", "delta", "conv")]
    return tuple(got[f"out_{name}{s}"] for name, s in order)
```
